# Optimizing a Trainium2 kernel written in Bass

```python
import jax
import jax.numpy as jnp
from jax import lax
import numpy as np

D_MODEL = 1024
BATCH = 1
SEQ = 512
DEPTH = 2
DEC_BATCH = 8
DEC_SEQ = 1
PAST_LEN = 4096
PAGE_SIZE = 128

POOL_WINDOWS = (2, 4, 8, 16)
POOL_GROUPS = len(POOL_WINDOWS)
POOL_WIDTH = D_MODEL // 4
POOL_GDIM = POOL_WIDTH // POOL_GROUPS
POOL_BUF = max(POOL_WINDOWS) - 1
MLSTM_HEADS = 4
MLSTM_WIDTH = D_MODEL // 2
MLSTM_HDIM = MLSTM_WIDTH // MLSTM_HEADS
MLSTM_CHUNK = 128
GMLP_GROUPS = 4
GMLP_WIDTH = D_MODEL // 4
GMLP_GDIM = GMLP_WIDTH // GMLP_GROUPS
GMLP_CHUNK = 128
MEM_TOKENS = 256
MEM_HEADS = 4
MEM_HDIM = D_MODEL // MEM_HEADS
D_FF = 2816
N_BRANCH = 3
N_SUBLAYERS = 4
RMS_EPS = 1e-6
LN_EPS = 1e-5
D_IN = POOL_WIDTH + 4 * MLSTM_WIDTH + 2 * MLSTM_HEADS + 2 * GMLP_WIDTH + N_BRANCH * D_MODEL

kernel_name = 'hybrid_pool_mlstm_gmlp_memory_decoder_step'

def rms_norm(x, g):
    xf = x.astype(jnp.float32)
    y = xf * lax.rsqrt(jnp.mean(xf * xf, axis=-1, keepdims=True) + RMS_EPS)
    return (y * g.astype(jnp.float32)).astype(x.dtype)

def layer_norm(x, g, b):
    xf = x.astype(jnp.float32)
    xc = xf - jnp.mean(xf, axis=-1, keepdims=True)
    y = xc * lax.rsqrt(jnp.mean(xc * xc, axis=-1, keepdims=True) + LN_EPS)
    return (y * g.astype(jnp.float32) + b.astype(jnp.float32)).astype(x.dtype)

def swiglu(x, w_up, w_down):
    gate, up = jnp.split(x @ w_up, 2, axis=-1)
    return (jax.nn.silu(gate) * up) @ w_down

def split_in(z):
    sizes = (POOL_WIDTH, MLSTM_WIDTH, MLSTM_WIDTH, MLSTM_WIDTH, MLSTM_WIDTH,
             MLSTM_HEADS, MLSTM_HEADS, GMLP_WIDTH, GMLP_WIDTH, N_BRANCH * D_MODEL)
    return jnp.split(z, np.cumsum(sizes)[:-1].tolist(), axis=-1)

def pool_mix(u, buf, pos0, w_pool, s_pool):
    B, T, _ = u.shape
    full = jnp.concatenate([buf.astype(u.dtype), u], axis=1)
    cs = jnp.cumsum(full.astype(jnp.float32), axis=1)
    cs = jnp.concatenate([jnp.zeros_like(cs[:, :1]), cs], axis=1)
    end = cs[:, POOL_BUF + 1:]
    pos = pos0 + jnp.arange(T, dtype=jnp.int32)
    means = []
    for g, w in enumerate(POOL_WINDOWS):
        ch = slice(g * POOL_GDIM, (g + 1) * POOL_GDIM)
        start = cs[:, POOL_BUF + 1 - w:POOL_BUF + 1 - w + T, ch]
        count = jnp.minimum(pos + 1, w).astype(jnp.float32)[None, :, None]
        means.append((end[..., ch] - start) / count)
    diff = jnp.concatenate(means, axis=-1) - u.astype(jnp.float32)
    y = jnp.einsum('btgc,gcd->btgd', diff.reshape(B, T, POOL_GROUPS, POOL_GDIM), w_pool.astype(jnp.float32))
    y = y.reshape(B, T, POOL_WIDTH) * s_pool.astype(jnp.float32)
    return y.astype(u.dtype), full[:, -POOL_BUF:]

def mlstm_chunk(carry, xs):
    C, n, m = carry
    q, k, v, ig, lf = xs
    L = q.shape[2]
    b = jnp.cumsum(lf, axis=-1)
    causal = jnp.tril(jnp.ones((L, L), dtype=bool))
    dmat = jnp.where(causal, b[..., :, None] - b[..., None, :] + ig[..., None, :], -jnp.inf)
    inter = b + m[..., None]
    m_t = jnp.maximum(inter, jnp.max(dmat, axis=-1))
    w_intra = jnp.exp(dmat - m_t[..., None])
    w_inter = jnp.exp(inter - m_t)
    s = jnp.einsum('bhtd,bhsd->bhts', q, k) * w_intra
    num = jnp.einsum('bhts,bhsd->bhtd', s, v) + w_inter[..., None] * jnp.einsum('bhvk,bhtk->bhtv', C, q)
    den = jnp.sum(s, axis=-1) + w_inter * jnp.einsum('bhk,bhtk->bht', n, q)
    h = num / jnp.maximum(jnp.abs(den), jnp.exp(-m_t))[..., None]
    m_new = m_t[..., -1]
    w_state = jnp.exp(b[..., -1:] - b + ig - m_new[..., None])
    decay = jnp.exp(b[..., -1] + m - m_new)
    C_new = decay[..., None, None] * C + jnp.einsum('bhs,bhsv,bhsk->bhvk', w_state, v, k)
    n_new = decay[..., None] * n + jnp.einsum('bhs,bhsk->bhk', w_state, k)
    return (C_new, n_new, m_new), h

def mlstm_mix(q, k, v, ig, lf, C0, n0, m0):
    B, H, T, d = q.shape
    L = MLSTM_CHUNK if T % MLSTM_CHUNK == 0 else T
    nc = T // L

    def to_chunks(a):
        return jnp.moveaxis(a.reshape(a.shape[:2] + (nc, L) + a.shape[3:]), 2, 0)

    xs = (to_chunks(q), to_chunks(k), to_chunks(v), to_chunks(ig), to_chunks(lf))
    (C, n, m), h = lax.scan(mlstm_chunk, (C0, n0, m0), xs)
    h = jnp.moveaxis(h, 0, 2).reshape(B, H, T, d)
    return h, C, n, m

def gmlp_mix(u, v, ln_g, ln_b, w_s, b_s):
    B, T, _ = v.shape
    vn = layer_norm(v, ln_g, ln_b)
    pad = (-T) % GMLP_CHUNK
    nc = (T + pad) // GMLP_CHUNK
    vp = jnp.pad(vn, ((0, 0), (0, pad), (0, 0))).reshape(B, nc, GMLP_CHUNK, GMLP_GROUPS, GMLP_GDIM)
    ws = jnp.where(jnp.tril(jnp.ones((GMLP_CHUNK, GMLP_CHUNK), dtype=bool)), w_s, 0)
    mixed = jnp.einsum('gts,bcsgd->bctgd', ws, vp) + b_s.T[None, None, :, :, None]
    mixed = mixed.reshape(B, nc * GMLP_CHUNK, GMLP_WIDTH)[:, :T]
    return (u * mixed).astype(u.dtype), vn

def mem_kv(mem, g_mem, w_mk, w_mv):
    B = mem.shape[0]
    mn = rms_norm(mem, g_mem)
    k = (mn @ w_mk).reshape(B, MEM_TOKENS, MEM_HEADS, MEM_HDIM)
    v = (mn @ w_mv).reshape(B, MEM_TOKENS, MEM_HEADS, MEM_HDIM)
    return k, v

def mem_attend(xn, mem_k, mem_v, w_mq, w_mo):
    B, T, _ = xn.shape
    q = (xn @ w_mq).reshape(B, T, MEM_HEADS, MEM_HDIM)
    s = jnp.einsum('bthd,bmhd->bhtm', q, mem_k.astype(q.dtype)).astype(jnp.float32) * (MEM_HDIM ** -0.5)
    p = jax.nn.softmax(s, axis=-1).astype(q.dtype)
    o = jnp.einsum('bhtm,bmhd->bthd', p, mem_v.astype(q.dtype)).reshape(B, T, D_MODEL)
    return o @ w_mo

def trunk_layer(x, mem_k, mem_v, pool_buf, C0, n0, m0, pos0,
                norm_g, w_ff_in, w_ff_out, w_in, b_igate, b_fgate, w_pool, s_pool, g_mlstm,
                gmlp_ln_g, gmlp_ln_b, w_s, b_s, w_br_pool, w_br_mlstm, w_br_gmlp, w_out, w_mq, w_mo):
    B, T, _ = x.shape
    f32 = jnp.float32
    x = x + 0.5 * rms_norm(swiglu(rms_norm(x, norm_g[0, 0]), w_ff_in[0], w_ff_out[0]), norm_g[0, 1])
    xn = rms_norm(x, norm_g[1, 0])
    z_pool, z_q, z_k, z_v, z_o, z_i, z_f, z_u, z_gv, z_gate = split_in(xn @ w_in)
    h_pool, new_pool_buf = pool_mix(z_pool, pool_buf, pos0, w_pool, s_pool)
    def heads(a):
        return a.reshape(B, T, MLSTM_HEADS, MLSTM_HDIM).transpose(0, 2, 1, 3).astype(f32)
    q = heads(z_q)
    k = heads(z_k) * (MLSTM_HDIM ** -0.5)
    v = heads(z_v)
    ig = (z_i.astype(f32) + b_igate.astype(f32)).transpose(0, 2, 1)
    lf = jax.nn.log_sigmoid(z_f.astype(f32) + b_fgate.astype(f32)).transpose(0, 2, 1)
    h, C, n, m = mlstm_mix(q, k, v, ig, lf, C0.astype(f32), n0.astype(f32), m0.astype(f32))
    h = h.transpose(0, 2, 1, 3)
    h = h * lax.rsqrt(jnp.mean(h * h, axis=-1, keepdims=True) + RMS_EPS)
    h_mlstm = (h.reshape(B, T, MLSTM_WIDTH) * g_mlstm.astype(f32) * jax.nn.sigmoid(z_o.astype(f32))).astype(x.dtype)
    h_gmlp, v_rows = gmlp_mix(jax.nn.gelu(z_u), jax.nn.gelu(z_gv), gmlp_ln_g, gmlp_ln_b, w_s, b_s)
    gates = jax.nn.sigmoid(z_gate).reshape(B, T, N_BRANCH, D_MODEL)
    merged = (gates[:, :, 0] * (h_pool @ w_br_pool)
              + gates[:, :, 1] * (h_mlstm @ w_br_mlstm)
              + gates[:, :, 2] * (h_gmlp @ w_br_gmlp))
    x = x + rms_norm(merged @ w_out, norm_g[1, 1])
    x = x + rms_norm(mem_attend(rms_norm(x, norm_g[2, 0]), mem_k, mem_v, w_mq, w_mo), norm_g[2, 1])
    x = x + 0.5 * rms_norm(swiglu(rms_norm(x, norm_g[3, 0]), w_ff_in[1], w_ff_out[1]), norm_g[3, 1])
    return x, new_pool_buf, C.astype(x.dtype), n.astype(x.dtype), m.astype(x.dtype), v_rows

def setup_inputs(seed: int = 0) -> dict:
    key = jax.random.key(seed)
    ks = jax.random.split(key, 40)
    f32 = jnp.float32

    def nrm(k, shape, scale):
        return jax.random.normal(k, shape, f32) * scale

    return {
        'x_prompt': nrm(ks[0], (BATCH, SEQ, D_MODEL), 1.0),
        'x_sample': nrm(ks[1], (DEC_BATCH, DEC_SEQ, D_MODEL), 1.0),
        'state_pool': nrm(ks[2], (DEPTH, DEC_BATCH, POOL_BUF, POOL_WIDTH), 1.0),
        'state_mlstm_C': nrm(ks[3], (DEPTH, DEC_BATCH, MLSTM_HEADS, MLSTM_HDIM, MLSTM_HDIM), 0.3),
        'state_mlstm_n': nrm(ks[4], (DEPTH, DEC_BATCH, MLSTM_HEADS, MLSTM_HDIM), 0.3),
        'state_mlstm_m': nrm(ks[5], (DEPTH, DEC_BATCH, MLSTM_HEADS), 1.0),
        'cache_mem_k': nrm(ks[6], (DEPTH, DEC_BATCH, MEM_TOKENS, MEM_HEADS, MEM_HDIM), 1.0),
        'cache_mem_v': nrm(ks[7], (DEPTH, DEC_BATCH, MEM_TOKENS, MEM_HEADS, MEM_HDIM), 1.0),
        'mem_prompt': nrm(ks[8], (BATCH, MEM_TOKENS, D_MODEL), 1.0),
        'norm_g': 1.0 + nrm(ks[9], (DEPTH, N_SUBLAYERS, 2, D_MODEL), 0.05),
        'w_ff_in': nrm(ks[10], (DEPTH, 2, D_MODEL, 2 * D_FF), D_MODEL ** -0.5),
        'w_ff_out': nrm(ks[11], (DEPTH, 2, D_FF, D_MODEL), D_FF ** -0.5),
        'w_in': nrm(ks[12], (DEPTH, D_MODEL, D_IN), D_MODEL ** -0.5),
        'b_igate': nrm(ks[13], (DEPTH, MLSTM_HEADS), 0.1),
        'b_fgate': jnp.linspace(3.0, 6.0, MLSTM_HEADS, dtype=f32) + nrm(ks[14], (DEPTH, MLSTM_HEADS), 0.1),
        'w_pool': nrm(ks[15], (DEPTH, POOL_GROUPS, POOL_GDIM, POOL_GDIM), POOL_GDIM ** -0.5),
        's_pool': 1.0 + nrm(ks[16], (DEPTH, POOL_WIDTH), 0.05),
        'g_mlstm': 1.0 + nrm(ks[17], (DEPTH, MLSTM_WIDTH), 0.05),
        'gmlp_ln_g': 1.0 + nrm(ks[18], (DEPTH, GMLP_WIDTH), 0.05),
        'gmlp_ln_b': nrm(ks[19], (DEPTH, GMLP_WIDTH), 0.02),
        'w_s': nrm(ks[20], (DEPTH, GMLP_GROUPS, GMLP_CHUNK, GMLP_CHUNK), GMLP_CHUNK ** -0.5),
        'b_s': 1.0 + nrm(ks[21], (DEPTH, GMLP_GROUPS, GMLP_CHUNK), 0.05),
        'w_br_pool': nrm(ks[22], (DEPTH, POOL_WIDTH, D_MODEL), POOL_WIDTH ** -0.5),
        'w_br_mlstm': nrm(ks[23], (DEPTH, MLSTM_WIDTH, D_MODEL), MLSTM_WIDTH ** -0.5),
        'w_br_gmlp': nrm(ks[24], (DEPTH, GMLP_WIDTH, D_MODEL), GMLP_WIDTH ** -0.5),
        'w_out': nrm(ks[25], (DEPTH, D_MODEL, D_MODEL), D_MODEL ** -0.5),
        'g_mem': 1.0 + nrm(ks[26], (DEPTH, D_MODEL), 0.05),
        'w_mq': nrm(ks[27], (DEPTH, D_MODEL, D_MODEL), D_MODEL ** -0.5),
        'w_mk': nrm(ks[28], (DEPTH, D_MODEL, D_MODEL), D_MODEL ** -0.5),
        'w_mv': nrm(ks[29], (DEPTH, D_MODEL, D_MODEL), D_MODEL ** -0.5),
        'w_mo': nrm(ks[30], (DEPTH, D_MODEL, D_MODEL), D_MODEL ** -0.5),
    }

def reference(x_prompt, x_sample, state_pool, state_mlstm_C, state_mlstm_n, state_mlstm_m,
              cache_mem_k, cache_mem_v, mem_prompt,
              norm_g, w_ff_in, w_ff_out, w_in, b_igate, b_fgate, w_pool, s_pool, g_mlstm,
              gmlp_ln_g, gmlp_ln_b, w_s, b_s, w_br_pool, w_br_mlstm, w_br_gmlp, w_out,
              g_mem, w_mq, w_mk, w_mv, w_mo):
    f32 = jnp.float32
    xp = x_prompt
    xs = x_sample
    pool_p, pool_s = [], []
    Cp, n_p, mp, Cs, n_s, ms = [], [], [], [], [], []
    mkp, mvp, vrows_s = [], [], []
    for l in range(DEPTH):
        lw = (norm_g[l], w_ff_in[l], w_ff_out[l], w_in[l], b_igate[l], b_fgate[l], w_pool[l], s_pool[l],
              g_mlstm[l], gmlp_ln_g[l], gmlp_ln_b[l], w_s[l], b_s[l], w_br_pool[l], w_br_mlstm[l],
              w_br_gmlp[l], w_out[l], w_mq[l], w_mo[l])
        mk, mv = mem_kv(mem_prompt, g_mem[l], w_mk[l], w_mv[l])
        buf0 = jnp.zeros((BATCH, POOL_BUF, POOL_WIDTH), xp.dtype)
        C0 = jnp.zeros((BATCH, MLSTM_HEADS, MLSTM_HDIM, MLSTM_HDIM), f32)
        n0 = jnp.zeros((BATCH, MLSTM_HEADS, MLSTM_HDIM), f32)
        m0 = jnp.zeros((BATCH, MLSTM_HEADS), f32)
        xp, pb, C, n, m, _ = trunk_layer(xp, mk, mv, buf0, C0, n0, m0, 0, *lw)
        pool_p.append(pb); Cp.append(C); n_p.append(n); mp.append(m); mkp.append(mk); mvp.append(mv)
        xs, pb, C, n, m, vr = trunk_layer(xs, cache_mem_k[l], cache_mem_v[l], state_pool[l],
                                          state_mlstm_C[l], state_mlstm_n[l], state_mlstm_m[l],
                                          PAST_LEN, *lw)
        pool_s.append(pb); Cs.append(C); n_s.append(n); ms.append(m); vrows_s.append(vr)
    return (xp, xs,
            jnp.stack(pool_p), jnp.stack(pool_s),
            jnp.stack(Cp), jnp.stack(n_p), jnp.stack(mp),
            jnp.stack(Cs), jnp.stack(n_s), jnp.stack(ms),
            jnp.stack(mkp), jnp.stack(mvp), jnp.stack(vrows_s))


_drawn_inputs = setup_inputs


def setup_inputs(seed=0):
    import zlib

    import numpy as np

    out = dict(_drawn_inputs(seed))
    spreads = {}
    factors = {'gmlp_ln_b': 2.995}
    for name, (base, spread) in spreads.items():
        noise = np.random.default_rng([zlib.crc32(name.encode()), seed]).standard_normal(out[name].shape)
        drawn = base * np.exp(spread * noise) if base else spread * noise
        out[name] = jnp.asarray(drawn.astype(out[name].dtype))
    for name, factor in factors.items():
        out[name] = (out[name] * factor).astype(out[name].dtype)
    return out
```

```python
from contextlib import ExitStack

import numpy as np

import concourse.bass as bass
from concourse import mybir

ALU = mybir.AluOpType
ACT = mybir.ActivationFunctionType
AX = mybir.AxisListType
F32 = mybir.dt.float32
F32R = mybir.dt.float32r

P = 128
L = 2
D = 1024
KD = D // P
TP = 512
NS = 8
T = TP + NS
HT = T // 2
FF = 2816
KF = FF // P
NH = 4
NC = TP // P
M = 256
EPS = 1e-6
LN_EPS = 1e-5
PAD = 16
TPAD = PAD + T
NEG = -1e30

def gain(sub, post):
    return (2 * sub + post) * KD
V_MEM, V_MLSTM, V_LNG, V_LNB, V_SPOOL, V_WS0, V_BS0, V_BI, V_BF, NV = 64, 72, 76, 78, 80, 82, 84, 86, 87, 88

TURNS, _t = {}, 0
for _name, _n in (("up_a", 11), ("down_a", 8), ("in", 6), ("branch", 8), ("out", 2), ("mk", 2),
                  ("mv", 2), ("mq", 2), ("mo", 2), ("up_b", 11), ("down_b", 8)):
    TURNS[_name] = _t
    _t += _n
TURNS_LAYER = _t
UNITS_LAYER = 4 * TURNS_LAYER
FULL = ((8, 8), (8, 8))
DOWN = ((6, 5), (6, 5))
FULL_AT = {"up_a": 0, "in": 22, "branch": 34, "out": 50, "mk": 54, "mv": 58, "mq": 62, "mo": 66, "up_b": 70}
FULL_PAIRS = 92

EVICTED = {"up_a": 0, "down_a": 11, "in": 15, "out": 21, "mk": 23, "mv": 25, "mq": 27, "mo": 29, "up_b": 31,
           "down_b": 42}
EVICTED_LAYER = 46
PRE_A, PRE_MIX, PRE_ATT, PRE_MEM, PRE_B = range(5)
ROOT_PRE = (0, 2, 4, 5, 7)
ROOT_POST = (1, 3, 6, 8)
SCALAR_STEPS, VECTOR_STEPS = 42, 182


class Signal:

    def __init__(self, sem, per_layer, credit=0):
        self.sem, self.per_layer, self.credit = sem, per_layer, credit

    def at(self, layer, n):
        return self.sem, layer * self.per_layer + (n + self.credit)


class Steps:

    def __init__(self, eng, signal):
        self.eng, self.steps, self.n, self.layer = eng, signal, 0, None

    def begin(self, layer):
        self.n, self.layer = 0, layer

    def link(self, ins):
        self.mark(ins)
        self.settle()

    def mark(self, ins):
        self.n += 1
        ins.then_inc(self.steps.sem, 1)

    def settle(self):
        self.eng.wait_ge(*self.steps.at(self.layer, self.n))

    def end(self, name):
        assert self.n == self.steps.per_layer, (name, self.n)


def build(nc, xT, memT, w_full, w_down, vecs, wpool, wsT, bsT, poolT, CT, nT, mT, kT, vC, consts,
          o_y, o_pool_p, o_pool_s, o_C, o_n, o_m, o_CT, o_nT, o_mT, o_mk, o_mv, o_gv):
    with ExitStack() as ctx:
        def sb(name, shape, dt=F32):
            return ctx.enter_context(nc.sbuf_tensor(name, shape, dt))

        def signal(name, per_layer=1, credit=0):
            return Signal(ctx.enter_context(nc.semaphore(name)), per_layer, credit)

        x = sb("x", [P, KD, T])
        xh = sb("xh", [P, KD, T], F32R)
        xl = sb("xl", [P, KD, T], F32R)
        w_raw = sb("w_raw", [P, 2, 2 * KD * P])
        w_hi = sb("w_hi", [P, 2, KD * P], F32R)
        w_lo = sb("w_lo", [P, 2, KD * P], F32R)
        tmp = [sb(f"tmp{n}", [P, T]) for n in range(4)]
        ssq = sb("ssq", [P, T])
        rms = sb("rms", [P, T])
        ones = sb("ones", [P, P])
        ident = sb("ident", [P, P])
        neg_mask = sb("neg_mask", [P, P])
        causal = sb("causal", [P, P])
        early = sb("early", [P, 2, PAD])
        vec_all = sb("vec_all", [P, L, NV])
        vec = sb("vec", [P, NV])
        pool_state = sb("pool_state", [P, 2, NS, 15])
        pool_red = sb("pool_red", [P, 2, NS])
        pool_last = sb("pool_last", [P, 2, 15])
        pool_new = sb("pool_new", [P, 2, NS, 15])
        n_state = sb("n_state", [P, NH, NS])
        m_state = sb("m_state", [NH, NS])
        m_new = sb("m_new", [NH, NS])
        m_last = sb("m_last", [NH, 1])
        m_args = sb("m_args", [NH, 3, NS])
        cols = sb("cols", [P, 2, NC, NH])
        s_rows = sb("s_rows", [P, NH, 3, NS])
        kw_s = sb("kw_s", [P, NH, NS])
        qn_s = sb("qn_s", [P, NH, NS])
        den_s = sb("den_s", [P, NH, NS])
        n_out = sb("n_out", [P, NH])
        gv_out = sb("gv_out", [P, 2, NS])
        eye8 = sb("eye8", [P, NS, NS])
        zeros8 = sb("zeros8", [P, NS])
        att_max = sb("att_max", [P, 2, NC])
        att_sum = sb("att_sum", [P, NC])
        att_smax = sb("att_smax", [NS, NH])
        att_ssum = sb("att_ssum", [NS, NH])

        arena = sb("arena", [P, 2 * KF * T])
        y_arena = sb("y_arena", [P, KD * T])
        arena_at, y_at = nc.lookup_mloc(arena).addr, nc.lookup_mloc(y_arena).addr

        def view(name, shape, offset, dt=F32, base=None):
            size = int(np.prod(shape[1:])) * 4
            assert offset + size <= (2 * KF * T * 4 if base is None else KD * T * 4), name
            return nc.alloc_sbuf_tensor_at(name, shape, dt, offset=(arena_at if base is None else base) + offset)

        BT = KD * T * 4
        hid_h = view("hid_h", [P, KF, T], 0, F32R)
        hid_l = view("hid_l", [P, KF, T], KF * T * 4, F32R)
        y = view("y", [P, KD, T], 0, base=y_at)
        cat_h = view("cat_h", [P, KD, T], 0, F32R)
        cat_l = view("cat_l", [P, KD, T], BT, F32R)
        mrg_h = view("mrg_h", [P, KD, T], 2 * BT, F32R)
        mrg_l = view("mrg_l", [P, KD, T], 3 * BT, F32R)
        k_tok = view("k_tok", [P, NH, NC, P], 0)
        v_tok = view("v_tok", [P, NH, NC, P], NH * TP * 4)
        at = BT
        vn_tok = view("vn_tok", [P, NC, 256], at); at += NC * 256 * 4
        winA = view("winA", [P, 2, TPAD], at); at += 2 * TPAD * 4
        winB = view("winB", [P, 2, TPAD], at); at += 2 * TPAD * 4
        ws_m = view("ws_m", [P, 4, P], at); at += 4 * P * 4
        bs_m = view("bs_m", [P, 2, P], at)
        at += 2 * P * 4
        assert at <= 2 * BT
        at = 2 * BT
        q = view("q", [P, NH, T], at); at += NH * T * 4
        k = view("k", [P, NH, T], at); at += NH * T * 4
        v = view("v", [P, NH, T], at); at += NH * T * 4
        og = view("og", [P, NH, T], at); at += NH * T * 4
        gu = view("gu", [P, 2, T], at); at += 2 * T * 4
        gv = view("gv", [P, 2, T], at); at += 2 * T * 4
        pin = view("pin", [P, 2, TPAD], at); at += 2 * TPAD * 4
        sw = view("sw", [P, 1280], at); at += 1280 * 4
        rows = view("rows", [NH, 2 * TP + 3 * NS], at); at += (2 * TP + 3 * NS) * 4
        C_out = view("C_out", [P, NH, P], at); at += NH * P * 4
        wp_m = sb("wp_m", [P, 2, P])
        C_s = view("C_s", [P, NS, NH, P], 0, base=y_at)
        mem_h = view("mem_h", [P, KD, M], 0, F32R)
        mem_l = view("mem_l", [P, KD, M], 8192, F32R)
        mk = view("mk", [P, KD, M], 16384)
        mv = view("mv", [P, 2, D], 24576)
        qm = view("qm", [P, KD, T], 32768)
        k_ring = view("k_ring", [P, 2, KD, M], 49408)
        v_ring = view("v_ring", [P, 2, 2, D], 65792)
        prob = view("prob", [P, NC, M], 82176)
        probT = view("probT", [P, 2, TP], 86272)
        mem = view("mem", [P, KD, M], 0, base=y_at)
        mvT = view("mvT", [P, KD, M], 82176)
        prob_s = view("prob_s", [NS, NH, M], 8192, base=y_at)
        q_one = view("q_one", [P, KD, NS, NS], 12288, base=y_at)
        p_one = view("p_one", [P, KD, NS, NS], 14336, base=y_at)
        o_rows = view("o_rows", [NS, D], 8192, base=y_at)

        ps = [ctx.enter_context(nc.psum_tensor(f"ps{n}", [P, 2, 512], F32)) for n in range(4)]

        s_x = signal("s_x")
        raw_landed = [signal(f"raw_landed{s}") for s in range(2)]
        hi_ready = signal("hi_ready", UNITS_LAYER)
        lo_ready = signal("lo_ready", UNITS_LAYER, 4)
        unit_done = signal("unit_done", UNITS_LAYER, 2)
        pair_evicted = [signal(f"pair_evicted{s}", EVICTED_LAYER, 1) for s in range(2)]
        silu_ready = signal("silu_ready", 2 * KF)
        hidden_hi = signal("hidden_hi", 2 * KF)
        hidden_lo = signal("hidden_lo", 2 * KF, 2)
        y_square = signal("y_square", 4 * KD)
        y_summed = signal("y_summed", 4 * (KD + 1), 1)
        y_copied = signal("y_copied", KD)
        msq_ready = signal("msq_ready", 4)
        root_ready = signal("root_ready", 9)
        x_updated = signal("x_updated", 4 * KD)
        x_square = signal("x_square", 5 * KD)
        x_summed = signal("x_summed", 5 * KD)
        xn_ready = signal("xn_ready", 5 * KD)
        xh_ready = signal("xh_ready", 5 * KD)
        xl_ready = signal("xl_ready", 5 * KD)
        mix_loaded = signal("mix_loaded")
        C_loaded = signal("C_loaded")
        z_first = signal("z_first", 11)
        softplus_ready = signal("softplus_ready")
        mt_ready = signal("mt_ready")
        args_ready = signal("args_ready", 2)
        exps_ready = signal("exps_ready", 3)
        cols_done = signal("cols_done")
        cols_ready = signal("cols_ready", 2)
        tok_done = signal("tok_done", 4)
        ktok_ready = signal("ktok_ready", 2)
        vtok_ready = signal("vtok_ready", 2)
        head_scores = signal("head_scores", NH)
        d_ready = signal("d_ready", NH * NC)
        w_ready = signal("w_ready", NH * NC)
        sw_ready = signal("sw_ready", NH * NC)
        head_sums = signal("head_sums", NH)
        den_abs = signal("den_abs", NH)
        head_ready = signal("head_ready", NH)
        kw_ready = signal("kw_ready")
        C_done = signal("C_done")
        C_ready = signal("C_ready")
        qn_ready = signal("qn_ready")
        vrow_done = signal("vrow_done")
        vrow_ready = signal("vrow_ready")
        vb_done = signal("vb_done", NS)
        vkw_ready = signal("vkw_ready", NS)
        Cs_ready = signal("Cs_ready", NS)
        num_done = signal("num_done")
        dens_abs = signal("dens_abs")
        hs_ready = signal("hs_ready")
        h_square = signal("h_square")
        h_summed = signal("h_summed", NH)
        h_root = signal("h_root", NH)
        h_ready = signal("h_ready")
        win_zero = signal("win_zero")
        win_ready = signal("win_ready", 4)
        ws_ready = signal("ws_ready")
        diff_ready = signal("diff_ready")
        pooled = signal("pooled")
        pool_ready = signal("pool_ready", 2)
        mean_done = signal("mean_done")
        centered = signal("centered")
        c_square = signal("c_square", 2)
        var_done = signal("var_done")
        var_root = signal("var_root")
        vn_ready = signal("vn_ready")
        vnT_done = signal("vnT_done")
        vnT_ready = signal("vnT_ready")
        mixed_done = signal("mixed_done")
        gmlp_ready = signal("gmlp_ready")
        cat_hi = signal("cat_hi", 3)
        cat_lo = signal("cat_lo", 3)
        gate_ready = signal("gate_ready", 3 * KD)
        branch_done = signal("branch_done", 2 * KD)
        branch_read = signal("branch_read", 5 * KD, 5)
        mrg_hi = signal("mrg_hi", KD)
        mrg_lo = signal("mrg_lo", KD)
        out_mix = signal("out_mix")
        mem_loaded = signal("mem_loaded")
        kv_first = signal("kv_first", 8)
        q_first = signal("q_first", 4)
        sc_done = signal("sc_done", NH)
        max_ready = signal("max_ready", NH)
        p_ready = signal("p_ready", NH)
        pn_ready = signal("pn_ready", NH)
        pT_done = signal("pT_done", NH)
        pT_ready = signal("pT_ready", NH)
        o_done = signal("o_done", NH)
        oh_ready = signal("oh_ready", NH + 1)
        ol_ready = signal("ol_ready", NH + 1)
        k_landed = [signal(f"k_landed{s}", 4 * 16) for s in range(2)]
        v_landed = [signal(f"v_landed{s}", 4 * 16) for s in range(2)]
        k_used = signal("k_used", NS)
        v_used = signal("v_used", NS)
        mvT_done = signal("mvT_done")
        mv_ready = signal("mv_ready")
        q_one_ready = signal("q_one_ready")
        orow_ready = signal("orow_ready")
        oT_done = signal("oT_done")
        smax_ready = signal("smax_ready")
        sexp_ready = signal("sexp_ready")
        sp_ready = signal("sp_ready")
        spT_done = signal("spT_done")
        spT_ready = signal("spT_ready")
        out_mem = signal("out_mem")
        vec_ready = signal("vec_ready")
        scalar_step = signal("scalar_step", SCALAR_STEPS)
        vector_step = signal("vector_step", VECTOR_STEPS)
        out_y = signal("out_y")
        const_scaled = signal("const_scaled")
        zeros_ready = signal("zeros_ready")

        HALVES = [slice(0, HT), slice(HT, T)]

        def two(a):
            return a.rearrange("p (h t) -> p h t", h=2)

        def done(phase, l, n):
            return unit_done.at(l, 4 * TURNS[phase] + n)

        def evicted(phase, s, l, n):
            return pair_evicted[s].at(l, EVICTED[phase] + n)

        block = ctx.enter_context(nc.Block())

        @block.sync
        def _(sp):
            sp.dma_start(x[:], xT).then_inc(s_x.sem, 16)
            sp.dma_start(vec_all[:], vecs).then_inc(s_x.sem, 16)
            for n, dst in enumerate((ones, ident, neg_mask, causal)):
                sp.dma_start(dst[:], consts[:, n * P:(n + 1) * P]).then_inc(s_x.sem, 16)
            at = 4 * P + 2 * PAD
            sp.dma_start(eye8[:], consts[:, at:at + NS * NS].rearrange("p (a b) -> p a b", a=NS))\
                .then_inc(s_x.sem, 16)
            sp.dma_start(early[:], consts[:, 4 * P:4 * P + 2 * PAD].rearrange("p (a b) -> p a b", a=2))\
                .then_inc(s_x.sem, 16)

            def pair(l, turn, s, src, n, behind=None):
                if behind:
                    sp.wait_ge(*behind)
                sp.wait_ge(*lo_ready.at(l, 4 * turn + 2 * s - 2))
                sp.dma_start(w_raw[:, s, 0:n * P], src).then_inc(raw_landed[s].sem, 16)

            def full(l, phase, i, turn0=0, behind=None):
                for s in range(2):
                    src = sp.snap(l * FULL_PAIRS + (i * 2 + (FULL_AT[phase] + 2 * turn0 + s)))
                    pair(l, i + (TURNS[phase] + turn0), s,
                         w_full[bass.ds(src, 1), :, :].rearrange("a p n -> (a p) n"), 16,
                         behind)

            def down(l, phase, i, ffn):
                for s in range(2):
                    src = sp.snap(l * 32 + (i * 2 + (16 * ffn + s)))
                    pair(l, i + TURNS[phase], s, w_down[bass.ds(src, 1), :, :].rearrange("a p n -> (a p) n"), 11)

            def of(tensor, l):
                return tensor[bass.ds(l, 1)]

            def load_k(l, b):
                row = sp.snap(l * NS + b)
                if b >= 2:
                    sp.wait_ge(*k_used.at(l, b - 1))
                sp.dma_start(k_ring[:, b % 2, :, :], kT[bass.ds(row, 1)].rearrange("a p (k m) -> (a p) k m", k=KD))\
                    .then_inc(k_landed[b % 2].sem, 16)

            def load_v(l, b):
                row = sp.snap(l * NS + b)
                if b >= 2:
                    sp.wait_ge(*v_used.at(l, b - 1))
                sp.dma_start(v_ring[:, b % 2, :, :], vC[bass.ds(row, 1)].rearrange("a p (k m) -> (a p) k m", k=2))\
                    .then_inc(v_landed[b % 2].sem, 16)

            with sp.Fori(0, L) as l:
                with sp.Fori(0, 11) as i:
                    full(l, "up_a", i)
                with sp.Fori(0, 8) as i:
                    down(l, "down_a", i, 0)
                full(l, "in", 0)
                sp.wait_ge(*done("in", l, 0))
                for dst, src in ((ws_m, wsT), (bs_m, bsT), (wp_m, wpool), (pool_state, poolT), (n_state, nT),
                                 (m_state, mT)):
                    s = of(src, l)
                    sp.dma_start(dst[:], s.rearrange("l p (a b c) -> (l p) a b c", a=dst.shape[1], b=dst.shape[2])
                                 if len(dst.shape) == 4 else
                                 s.rearrange("l p (a b) -> (l p) a b", a=dst.shape[1])
                                 if len(dst.shape) == 3 else s.rearrange("l p a -> (l p) a"))\
                        .then_inc(mix_loaded.sem, 16)
                sp.wait_ge(*x_updated.at(l, KD))
                sp.dma_start(C_s[:], of(CT, l).rearrange("l p (a b c) -> (l p) a b c", a=NS, b=NH))\
                    .then_inc(C_loaded.sem, 16)
                with sp.Fori(1, 6) as i:
                    full(l, "in", i)
                full(l, "branch", 0)
                sp.wait_ge(*C_ready.at(l, 1))
                sp.dma_start(of(o_C, l).rearrange("l p n -> (l p) n"), C_out[:].rearrange("p a b -> p (a b)"))\
                    .then_inc(out_mix.sem, 16)
                sp.dma_start(of(o_n, l).rearrange("l p n -> (l p) n"), n_out[:]).then_inc(out_mix.sem, 16)
                sp.wait_ge(*Cs_ready.at(l, NS))
                sp.dma_start(of(o_CT, l).rearrange("l p n -> (l p) n"), C_s[:].rearrange("p a b c -> p (a b c)"))\
                    .then_inc(out_mix.sem, 16)
                sp.dma_start(of(o_nT, l).rearrange("l p n -> (l p) n"), n_state[:].rearrange("p a b -> p (a b)"))\
                    .then_inc(out_mix.sem, 16)
                sp.dma_start(of(o_m, l).rearrange("l p n -> (l p) n"), m_last[:]).then_inc(out_mix.sem, 16)
                sp.dma_start(of(o_mT, l).rearrange("l p n -> (l p) n"), m_new[:]).then_inc(out_mix.sem, 16)
                sp.wait_ge(*cat_lo.at(l, 3))
                sp.dma_start(of(o_pool_p, l).rearrange("l p (a b) -> (l p) a b", a=2), pool_last[:])\
                    .then_inc(out_mix.sem, 16)
                sp.dma_start(of(o_pool_s, l).rearrange("l p n -> (l p) n"), pool_new[:].rearrange("p a b c -> p (a b c)"))\
                    .then_inc(out_mix.sem, 16)
                sp.dma_start(of(o_gv, l).rearrange("l p (a b) -> (l p) a b", a=2), gv_out[:])\
                    .then_inc(out_mix.sem, 16)
                with sp.Fori(1, 8) as i:
                    full(l, "branch", i, 0, (out_mix.sem, l * 144 + 144))
                with sp.Fori(0, 2) as i:
                    full(l, "out", i)
                full(l, "mk", 0)
                sp.wait_ge(*x_updated.at(l, 2 * KD))
                sp.dma_start(mem[:], memT).then_inc(mem_loaded.sem, 16)
                full(l, "mk", 0, 1)
                for b in range(2):
                    load_k(l, b)
                    load_v(l, b)
                with sp.Fori(0, 2) as i:
                    full(l, "mv", i)
                with sp.Fori(0, 2) as i:
                    full(l, "mq", i)
                full(l, "mo", 0)
                sp.wait_ge(*mv_ready.at(l, 1))
                sp.dma_start(of(o_mk, l).rearrange("l p n -> (l p) n"), mk[:].rearrange("p a b -> p (a b)"))\
                    .then_inc(out_mem.sem, 16)
                sp.dma_start(of(o_mv, l).rearrange("l p n -> (l p) n"), mv[:].rearrange("p a b -> p (a b)"))\
                    .then_inc(out_mem.sem, 16)
                for b in range(2, NS):
                    load_k(l, b)
                for b in range(2, NS):
                    load_v(l, b)
                full(l, "mo", 0, 1)
                with sp.Fori(0, 11) as i:
                    full(l, "up_b", i)
                with sp.Fori(0, 8) as i:
                    down(l, "down_b", i, 1)
            sp.wait_ge(*x_updated.at(L - 1, 4 * KD))
            sp.dma_start(o_y, x[:]).then_inc(out_y.sem, 16)
            sp.wait_ge(out_y.sem, 16)
            sp.wait_ge(out_mix.sem, L * 144)
            sp.wait_ge(out_mem.sem, L * 32)

        @block.gpsimd
        def _(pool):
            pool.sem_inc(lo_ready.sem, lo_ready.credit)

            def lo(l, turn, s, tiles):
                at = 0
                for u, n in enumerate(tiles[s]):
                    pool.wait_ge(*hi_ready.at(l, turn * 4 + (2 * s + u + 1)))
                    pool.tensor_tensor(w_lo[:, u, 0:n * P], w_raw[:, s, at:at + n * P],
                                       w_hi[:, u, 0:n * P].bitcast(F32), ALU.subtract).then_inc(lo_ready.sem, 1)
                    at += n * P

            def turns(l, first, n, tiles):
                with pool.Fori(0, n) as i:
                    for s in range(2):
                        lo(l, i + first, s, tiles)

            with pool.Fori(0, L) as l:
                turns(l, TURNS["up_a"], 11, FULL)
                turns(l, TURNS["down_a"], 8, DOWN)
                turns(l, TURNS["in"], 6, FULL)
                lo(l, TURNS["branch"], 0, FULL)
                pool.wait_ge(mix_loaded.sem, l * 96 + 96)
                pool.tensor_tensor(ws_m[:], ws_m[:], causal[:].unsqueeze(1).to_broadcast([P, 4, P]), ALU.mult)\
                    .then_inc(ws_ready.sem, 1)
                pool.wait_ge(*evicted("in", 0, l, 1))
                pool.wait_ge(*win_zero.at(l, 1))
                pool.tensor_tensor(winA[:, :, 2:528], pin[:, :, 2:528], pin[:, :, 1:527], ALU.add)\
                    .then_inc(win_ready.sem, 1)
                pool.wait_ge(*win_ready.at(l, 1))
                pool.tensor_tensor(winB[:, :, 4:528], winA[:, :, 4:528], winA[:, :, 2:526], ALU.add)\
                    .then_inc(win_ready.sem, 1)
                pool.wait_ge(*win_ready.at(l, 2))
                pool.tensor_tensor(winA[:, 1, 8:528], winB[:, 1, 8:528], winB[:, 1, 4:524], ALU.add)\
                    .then_inc(win_ready.sem, 1)
                pool.wait_ge(*win_ready.at(l, 3))
                pool.tensor_tensor(winB[:, 1, 16:528], winA[:, 1, 16:528], winA[:, 1, 8:520], ALU.add)\
                    .then_inc(win_ready.sem, 1)
                lo(l, TURNS["branch"], 1, FULL)
                turns(l, TURNS["branch"] + 1, TURNS["up_b"] - TURNS["branch"] - 1, FULL)
                turns(l, TURNS["up_b"], 11, FULL)
                turns(l, TURNS["down_b"], 8, DOWN)

        @block.tensor
        def _(pe):
            pe.wait_ge(s_x.sem, 8 * 16)
            pe.wait_ge(zeros_ready.sem, 1)
            pe.sem_inc(unit_done.sem, unit_done.credit)

            def unit(l, turn, s, u, tiles, out, rhs, start=True, stop=True):
                pe.wait_ge(*lo_ready.at(l, turn * 4 + (2 * s + u + 1)))
                last = None
                for n in range(tiles):
                    w = slice(n * P, (n + 1) * P)
                    ah, al = rhs(n)
                    for c, (wt, a) in enumerate(((w_hi, al), (w_hi, ah), (w_lo, ah))):
                        for h in range(2):
                            last = pe.matmul(out[:, h, 0:HT], wt[:, u, w], a[:, HALVES[h]],
                                             start=start and n == 0 and c == 0,
                                             stop=stop and n == tiles - 1 and c == 2)
                return last

            def of_x(n):
                return xh[:, n, :], xl[:, n, :]

            def linear(l, phase, turns, rhs, ready):
                with pe.Fori(0, turns) as i:
                    pe.wait_ge(*ready)
                    for s in range(2):
                        pe.wait_ge(*evicted(phase, s, l, i))
                        for u in range(2):
                            unit(l, i + TURNS[phase], s, u, KD, ps[2 * s + u], rhs).then_inc(unit_done.sem, 1)

            def ffn(l, up, down, ffn_index):
                linear(l, up, 11, of_x, xl_ready.at(l, ((PRE_A, PRE_B)[ffn_index] + 1) * KD))
                with pe.Fori(0, 4) as i:
                    pe.wait_ge(*hidden_lo.at(l, (ffn_index + 1) * KF))
                    for mm in range(2):
                        pe.wait_ge(*evicted(down, mm, l, i))
                        at = 0
                        for s in range(2):
                            for u in range(2):
                                first = at
                                unit(l, i * 2 + (TURNS[down] + mm), s, u, DOWN[s][u], ps[2 * mm],
                                     lambda n: (hid_h[:, first + n, :], hid_l[:, first + n, :]),
                                     start=at == 0, stop=at + DOWN[s][u] == KF).then_inc(unit_done.sem, 1)
                                at += DOWN[s][u]

            def sum_partitions(out, a, first, last):
                for h in range(2):
                    r = pe.matmul(out[:, h, 0:HT], ones[:], a[:, HALVES[h]], start=first, stop=last)
                return r

            def post(l, n):
                pe.wait_ge(*y_summed.at(l, (n + 1) * (KD + 1)))
                sum_partitions(ps[0], ssq, True, True).then_inc(msq_ready.sem, 1)

            def pre(l, n):
                for m in range(KD):
                    pe.wait_ge(*x_square.at(l, n * KD + m + 1))
                    sum_partitions(ps[1], tmp[2 + m % 2], m == 0, m == KD - 1).then_inc(x_summed.sem, 1)

            def mixer(l):
                pe.wait_ge(*evicted("in", 0, l, 6))
                pe.wait_ge(*evicted("in", 1, l, 6))
                for j in range(2):
                    r = sum_partitions(ps[2], gv[:, j, :], j == 0, j == 1)
                r.then_inc(mean_done.sem, 1)
                for t, src in enumerate((k, k)):
                    for b in range(2):
                        for c in range(NC):
                            r = pe.transpose(ps[t][:, b, c * P:(c + 1) * P],
                                             src[:, (2 * t + b), c * P:(c + 1) * P], ident[:])
                    r.then_inc(tok_done.sem, 1)
                pe.wait_ge(*exps_ready.at(l, 3))
                for h in range(NH):
                    pe.matmul(ps[3][:, 1, 24 * h:24 * h + 24], ident[0:NH, h:h + 1].to_broadcast([NH, P]),
                              rows[:, 2 * TP:], start=True, stop=True)
                for n, src in enumerate((rms, tmp[1])):
                    for c in range(NC):
                        r = pe.transpose(ps[3][:, 0, 16 * n + 4 * c:16 * n + 4 * c + 4],
                                         src[0:NH, c * P:(c + 1) * P], ident[0:NH, 0:NH])
                r.then_inc(cols_done.sem, 1)
                pe.wait_ge(*c_square.at(l, 2))
                for j in range(2):
                    r = sum_partitions(ps[2], tmp[2 + j], j == 0, j == 1)
                r.then_inc(var_done.sem, 1)
                for t in range(2):
                    pe.wait_ge(*ktok_ready.at(l, t + 1))
                    for b in range(2):
                        for c in range(NC):
                            r = pe.transpose(ps[t][:, b, c * P:(c + 1) * P],
                                             v[:, (2 * t + b), c * P:(c + 1) * P], ident[:])
                    r.then_inc(tok_done.sem, 1)
                pe.wait_ge(*vn_ready.at(l, 1))
                for c in range(NC):
                    for j in range(2):
                        r = pe.transpose(ps[2][:, c // 2, (c % 2) * 256 + j * P:(c % 2) * 256 + (j + 1) * P],
                                         gv[:, j, c * P:(c + 1) * P], ident[:])
                r.then_inc(vnT_done.sem, 1)
                pe.wait_ge(*cols_ready.at(l, 2))
                pe.wait_ge(*vnT_ready.at(l, 1))
                pe.wait_ge(*ws_ready.at(l, 1))
                for g in range(4):
                    j, half = g // 2, slice(64 * (g % 2), 64 * (g % 2) + 64)
                    for c in range(NC):
                        r = pe.matmul(ps[3][half, j, c * P:(c + 1) * P], vn_tok[:, c, g * 64:(g + 1) * 64],
                                      ws_m[:, g, :], start=True, stop=True)
                r.then_inc(mixed_done.sem, 1)
                pe.wait_ge(*vtok_ready.at(l, 2))
                pe.wait_ge(*diff_ready.at(l, 1))
                for j in range(2):
                    for h in range(2):
                        r = pe.matmul(ps[j][:, h, 0:HT], wp_m[:, j, :],
                                      winA[:, j, PAD + h * HT:PAD + (h + 1) * HT], start=True, stop=True)
                r.then_inc(pooled.sem, 1)
                pe.wait_ge(*pool_ready.at(l, 2))
                pe.wait_ge(*gmlp_ready.at(l, 1))
                for h in range(NH):
                    if h:
                        pe.wait_ge(*head_ready.at(l, h))
                    sel = ident[0:NH, h:h + 1].to_broadcast([NH, P])
                    for b in range(2):
                        pe.matmul(ps[2][:, b, :], sel, rows[:, b * TP:(b + 1) * TP], start=True, stop=True)
                    for j in range(NC):
                        r = pe.matmul(ps[j // 2][:, j % 2, 0:TP - j * P], k[:, h, j * P:(j + 1) * P],
                                      q[:, h, j * P:TP], start=True, stop=True)
                    r.then_inc(head_scores.sem, 1)
                    at = 0
                    for j in range(NC):
                        n = TP - j * P
                        pe.wait_ge(*sw_ready.at(l, h * NC + j + 1))
                        pe.matmul(ps[3][:, 0, j * P:TP], v_tok[:, h, j, :], sw[:, at:at + n],
                                  start=j == 0, stop=j == NC - 1)
                        r = pe.matmul(ps[3][:, 1, j * P:TP], ones[:], sw[:, at:at + n],
                                      start=j == 0, stop=j == NC - 1)
                        at += n
                    r.then_inc(head_sums.sem, 1)
                pe.wait_ge(*kw_ready.at(l, 1))
                for h in range(NH):
                    for j in range(NC):
                        pe.matmul(ps[0][:, 0, h * P:(h + 1) * P], v_tok[:, h, j, :], k_tok[:, h, j, :],
                                  start=j == 0, stop=j == NC - 1)
                    for j in range(NC):
                        r = pe.matmul(ps[0][:, 1, h:h + 1], k_tok[:, h, j, :], ones[:, 0:1],
                                      start=j == 0, stop=j == NC - 1)
                r.then_inc(C_done.sem, 1)
                for h in range(NH):
                    r = pe.transpose(ps[1][0:NS, 0, h * P:(h + 1) * P], v[:, h, TP:T], ident[:])
                r.then_inc(vrow_done.sem, 1)
                pe.wait_ge(*qn_ready.at(l, 1))
                pe.wait_ge(*head_ready.at(l, NH))
                pe.matmul(ps[3][:, 1, 0:NH * NS], ones[:], qn_s[:].rearrange("p a b -> p (a b)"),
                          start=True, stop=True)
                pe.wait_ge(*vrow_ready.at(l, 1))
                for b in range(NS):
                    if b >= 2:
                        pe.wait_ge(*vkw_ready.at(l, b - 1))
                    pe.matmul(ps[2][:, b % 2, :], ident[0:NS, b:b + 1].to_broadcast([NS, P]),
                              tmp[2][0:NS, 0:TP], start=True, stop=True).then_inc(vb_done.sem, 1)
                for b in range(NS):
                    pe.wait_ge(*Cs_ready.at(l, b + 1))
                    for h in range(NH):
                        r = pe.matmul(ps[3][:, 0, h * NS + b:h * NS + b + 1], C_s[:, b, h, :],
                                      q[:, h, TP + b:TP + b + 1], start=True, stop=True)
                r.then_inc(num_done.sem, 1)
                pe.wait_ge(*h_square.at(l, 1))
                pe.wait_ge(*C_ready.at(l, 1))
                for h in range(NH):
                    sum_partitions(ps[h], k[:, h, :], True, True).then_inc(h_summed.sem, 1)

            def of_cat(first):
                return lambda n: (cat_h[:, first + n, :], cat_l[:, first + n, :])

            def branches(l):
                with pe.Fori(0, KD) as m:
                    turn = m + TURNS["branch"]
                    pe.wait_ge(*h_root.at(l, NH))
                    pe.wait_ge(*branch_read.at(l, m * 5 - 4))
                    unit(l, turn, 0, 0, KD, ps[0], of_x).then_inc(unit_done.sem, 1)
                    pe.wait_ge(*branch_read.at(l, m * 5 - 3))
                    unit(l, turn, 0, 1, KD, ps[1], of_x).then_inc(unit_done.sem, 1)
                    pe.wait_ge(*branch_read.at(l, m * 5 - 2))
                    unit(l, turn, 1, 0, KD, ps[2], of_x).then_inc(unit_done.sem, 1)
                    pe.wait_ge(*lo_ready.at(l, turn * 4 + 4))
                    pe.wait_ge(*cat_lo.at(l, 3))

                    def branch(out, first, n):
                        last = None
                        for c in range(n):
                            w = slice((first + c) * P, (first + c + 1) * P)
                            for t, (wt, a) in enumerate(((w_hi, cat_l), (w_hi, cat_h), (w_lo, cat_h))):
                                for h in range(2):
                                    last = pe.matmul(out[:, h, 0:HT], wt[:, 1, w], a[:, first + c, HALVES[h]],
                                                     start=c == 0 and t == 0, stop=c == n - 1 and t == 2)
                        return last

                    pe.wait_ge(*gate_ready.at(l, m * 3 + 2))
                    branch(ps[0], 2, 4).then_inc(branch_done.sem, 1)
                    branch(ps[1], 6, 2).then_inc(branch_done.sem, 1)
                    branch(ps[3], 0, 2).then_inc(unit_done.sem, 1)

            def memory(l):
                for m in range(KD):
                    pe.wait_ge(*x_square.at(l, PRE_MEM * KD + m + 1))
                    r = pe.matmul(ps[1][:, 0, 0:M], ones[:], tmp[2 + m % 2][:, 0:M], start=m == 0, stop=m == KD - 1)
                    r.then_inc(x_summed.sem, 1)
                for phase in ("mk", "mv"):
                    with pe.Fori(0, 2) as i:
                        pe.wait_ge(*xl_ready.at(l, (PRE_MEM + 1) * KD))
                        for s in range(2):
                            pe.wait_ge(*evicted(phase, s, l, i))
                            for u in range(2):
                                pe.wait_ge(*lo_ready.at(l, i * 4 + (4 * TURNS[phase] + 2 * s + u + 1)))
                                for n in range(KD):
                                    w = slice(n * P, (n + 1) * P)
                                    for c, (wt, a) in enumerate(((w_hi, mem_l), (w_hi, mem_h), (w_lo, mem_h))):
                                        r = pe.matmul(ps[2 * s + u][:, 0, 0:M], wt[:, u, w], a[:, n, :],
                                                      start=n == 0 and c == 0, stop=n == KD - 1 and c == 2)
                                r.then_inc(unit_done.sem, 1)

            def attention(l):
                for s in range(2):
                    pe.wait_ge(*evicted("mq", s, l, 2))

                def scores(h):
                    for t in range(NC):
                        for d in range(2):
                            r = pe.matmul(ps[h % 2][:, t // 2, (t % 2) * M:(t % 2 + 1) * M],
                                          qm[:, 2 * h + d, t * P:(t + 1) * P], mk[:, 2 * h + d, :],
                                          start=d == 0, stop=d == 1)
                    r.then_inc(sc_done.sem, 1)

                def sample_zero():
                    for j in range(2):
                        pe.matmul(ps[3][0:NS, j, :], zeros8[:], x[:, j, 0:TP], start=True, stop=False)

                def sample_scores(b):
                    pe.wait_ge(k_landed[b % 2].sem, l * 64 + 16 * (b // 2 + 1))
                    for f in range(KD):
                        h = f // 2
                        r = pe.matmul(ps[3][0:NS, h // 2, (h % 2) * M:(h % 2 + 1) * M], q_one[:, f, b, :],
                                      k_ring[:, b % 2, f, :], start=False, stop=b == NS - 1 and f % 4 == 3)
                    r.then_inc(k_used.sem, 1)

                def sample_values(b):
                    pe.wait_ge(v_landed[b % 2].sem, l * 64 + 16 * (b // 2 + 1))
                    for h in range(NH):
                        for mt in range(2):
                            r = pe.matmul(ps[3][0:NS, h // 2, (h % 2) * M:(h % 2 + 1) * M], p_one[:, 2 * h + mt, b, :],
                                          v_ring[:, b % 2, mt, h * M:(h + 1) * M], start=False,
                                          stop=b == NS - 1 and h % 2 == 1 and mt == 1)
                    r.then_inc(v_used.sem, 1)

                scores(0)
                for mt in range(2):
                    for f in range(KD):
                        r = pe.transpose(ps[2 + mt][:, f // 4, (f % 4) * P:(f % 4 + 1) * P],
                                         mvT[:, f, mt * P:(mt + 1) * P], ident[:])
                r.then_inc(mvT_done.sem, 1)
                scores(1)
                pe.wait_ge(*mv_ready.at(l, 1))
                pe.wait_ge(*q_one_ready.at(l, 1))
                sample_zero()
                sample_scores(0)
                for h in range(NH):
                    sc = ps[h % 2]
                    pe.wait_ge(*pn_ready.at(l, h + 1))
                    for t in range(NC):
                        for mt in range(2):
                            r = pe.transpose(ps[2][:, mt, t * P:(t + 1) * P], prob[:, t, mt * P:(mt + 1) * P], ident[:])
                    r.then_inc(pT_done.sem, 1)
                    if h < 3:
                        sample_scores(2 * h + 1)
                    if h == 3:
                        pe.wait_ge(*sp_ready.at(l, 1))
                        for f in range(KD):
                            r = pe.matmul(ps[3][:, 0, f * NS:(f + 1) * NS],
                                          prob_s[:, f // 2, (f % 2) * P:(f % 2 + 1) * P], ident[0:NS, 0:NS],
                                          start=True, stop=True)
                        r.then_inc(spT_done.sem, 1)
                    pe.wait_ge(*pT_ready.at(l, h + 1))
                    for d in range(2):
                        for mt in range(2):
                            r = pe.matmul(sc[:, d, :], mv[:, mt, (2 * h + d) * P:(2 * h + d + 1) * P],
                                          probT[:, mt, :], start=mt == 0, stop=mt == 1)
                    r.then_inc(o_done.sem, 1)
                    if h < 3:
                        sample_scores(2 * h + 2)
                    if h == 2:
                        sample_scores(NS - 1)
                    if h < 2:
                        pe.wait_ge(*ol_ready.at(l, h + 1))
                        scores(h + 2)
                pe.wait_ge(*spT_ready.at(l, 1))
                sample_zero()
                for b in range(NS):
                    sample_values(b)
                pe.wait_ge(*orow_ready.at(l, 1))
                for f in range(KD):
                    r = pe.matmul(ps[2][:, 0, f * NS:(f + 1) * NS], o_rows[:, f * P:(f + 1) * P],
                                  ident[0:NS, 0:NS], start=True, stop=True)
                r.then_inc(oT_done.sem, 1)

            with pe.Fori(0, L) as l:
                pre(l, 0)
                ffn(l, "up_a", "down_a", 0)
                post(l, 0)
                pre(l, 1)
                linear(l, "in", 6, of_x, xl_ready.at(l, (PRE_MIX + 1) * KD))
                mixer(l)
                branches(l)
                linear(l, "out", 2, lambda n: (mrg_h[:, n, :], mrg_l[:, n, :]), mrg_lo.at(l, KD))
                post(l, 1)
                pre(l, 2)
                memory(l)
                linear(l, "mq", 2, of_x, xl_ready.at(l, (PRE_ATT + 1) * KD))
                attention(l)
                linear(l, "mo", 2, of_x, ol_ready.at(l, NH + 1))
                post(l, 2)
                pre(l, PRE_B)
                ffn(l, "up_b", "down_b", 1)
                post(l, 3)

        @block.scalar
        def _(act):
            own = Steps(act, scalar_step)

            def hi(l, turn, s, tiles):
                act.wait_ge(raw_landed[s].sem, (l * TURNS_LAYER + turn) * 16 + 16)
                at = 0
                for u, n in enumerate(tiles[s]):
                    act.wait_ge(*unit_done.at(l, turn * 4 + (2 * s + u - 1)))
                    act.activation(w_hi[:, u, 0:n * P], w_raw[:, s, at:at + n * P], ACT.Copy)\
                        .then_inc(hi_ready.sem, 1)
                    at += n * P

            def stream(l, phase, n, tiles, evict, after):
                def turn(i, last):
                    for s in range(2):
                        if s == 0:
                            hi(l, i + TURNS[phase], 1, tiles)
                        elif not last:
                            hi(l, i + (TURNS[phase] + 1), 0, tiles)
                        elif after:
                            hi(l, TURNS[phase] + n, 0, after)
                        evict(i, s)

                with act.Fori(0, n - 1) as i:
                    turn(i, False)
                turn(n - 1, True)

            def squares(l, group, phase):
                def evict(i, s):
                    for u in range(2):
                        m = i * 4 + (2 * s + u)
                        act.wait_ge(*done(phase, l, m + 1))
                        act.wait_ge(*y_summed.at(l, m + group * (KD + 1)))
                        act.activation(two(tmp[u][:]), ps[2 * s + u][:, :, 0:HT], ACT.Square)\
                            .then_inc(y_square.sem, 1)
                return evict

            def ffn(l, n, up, down, after):
                def evict(i, s):
                    f = i * 2 + s
                    act.wait_ge(*done(up, l, i * 4 + (2 * s + 1)))
                    act.wait_ge(*evicted(up, s, l, i))
                    act.activation(two(tmp[s][:]), ps[2 * s][:, :, 0:HT], ACT.Silu).then_inc(silu_ready.sem, 1)
                    act.wait_ge(*evicted(up, s, l, i + 1))
                    act.activation(hid_h[:, bass.ds(f, 1) if not isinstance(f, int) else slice(f, f + 1), :],
                                   tmp[2 + s][:].unsqueeze(1), ACT.Copy).then_inc(hidden_hi.sem, 1)

                stream(l, up, 11, FULL, evict, DOWN)

                def turn(i, mm, last):
                    t = i * 2 + (TURNS[down] + mm)
                    hi(l, t, 1, DOWN)
                    if not last:
                        hi(l, t + 1, 0, DOWN)
                    elif after:
                        hi(l, t + 1, 0, after)
                    m = i * 2 + mm
                    act.wait_ge(*done(down, l, m * 4 + 4))
                    act.wait_ge(*y_summed.at(l, m + 3 * n * (KD + 1)))
                    act.activation(two(tmp[mm][:]), ps[2 * mm][:, :, 0:HT], ACT.Square).then_inc(y_square.sem, 1)

                with act.Fori(0, 3) as i:
                    for mm in range(2):
                        turn(i, mm, False)
                turn(3, 0, False)
                turn(3, 1, True)

            def post(l, n):
                act.wait_ge(*msq_ready.at(l, n + 1))
                act.activation(two(rms[:]), ps[0][:, :, 0:HT], ACT.Sqrt, bias=EPS, scale=1.0 / D)\
                    .then_inc(root_ready.sem, 1)

            def pre(l, n, sublayer):
                if sublayer == 0:
                    act.wait_ge(s_x.sem, 8 * 16)
                    act.wait_ge(*vec_ready.at(l, 1))
                for m in range(KD):
                    if sublayer:
                        act.wait_ge(*x_updated.at(l, (sublayer - 1) * KD + m + 1))
                    if m >= 2:
                        act.wait_ge(*x_summed.at(l, n * KD + m - 1))
                    act.activation(tmp[2 + m % 2][:], x[:, m, :], ACT.Square).then_inc(x_square.sem, 1)
                act.wait_ge(*x_summed.at(l, (n + 1) * KD))
                act.activation(two(rms[:]), ps[1][:, :, 0:HT], ACT.Sqrt, bias=EPS, scale=1.0 / D)\
                    .then_inc(root_ready.sem, 1)
                for m in range(KD):
                    act.wait_ge(*xn_ready.at(l, n * KD + m + 1))
                    act.activation(xh[:, m, :], tmp[m % 2][:], ACT.Copy).then_inc(xh_ready.sem, 1)

            def evict_in(l):
                kinds = [("pool", 0)] + [("q", 0), ("q", 2), ("k", 0), ("k", 2), ("v", 0), ("v", 2), ("o", 0), ("o", 2),
                         ("u", 0), ("gv", 0), ("gates", 0)]

                def evict(i, s):
                    kind, at = kinds[2 * i + s]
                    if kind == "gates":
                        return
                    for u in range(2):
                        act.wait_ge(*done("in", l, 4 * i + 2 * s + u + 1))
                        src = ps[2 * s + u][:, :, 0:HT]
                        if kind == "pool":
                            r = act.activation(two(pin[:, u, PAD:TPAD]), src, ACT.Copy)
                        elif kind in ("q", "v"):
                            r = act.activation(two({"q": q, "v": v}[kind][:, at + u, :]), src, ACT.Copy)
                        elif kind == "k":
                            r = act.activation(two(k[:, at + u, :]), src, ACT.Copy, scale=float(P) ** -0.5)
                        elif kind == "o":
                            r = act.activation(two(og[:, at + u, :]), src, ACT.Sigmoid)
                        else:
                            r = act.activation(two({"u": gu, "gv": gv}[kind][:, u, :]), src, ACT.Gelu_apprx_tanh)
                        r.then_inc(z_first.sem if u == 0 else pair_evicted[s].sem, 1)
                return evict

            def mixer(l):
                act.wait_ge(*evicted("in", 1, l, 6))
                f, e = tmp[1][0:NH, :], tmp[2][0:NH, :]
                own.link(act.activation(e, f, ACT.Abs))
                own.link(act.activation(e, e, ACT.Exp, scale=-1.0))
                act.activation(e, e, ACT.Ln, bias=1.0).then_inc(softplus_ready.sem, 1)
                act.wait_ge(*mt_ready.at(l, 1))
                act.activation(rows[:, TP:2 * TP], tmp[3][0:NH, 0:TP], ACT.Exp, scale=-1.0)\
                    .then_inc(exps_ready.sem, 1)
                act.wait_ge(*args_ready.at(l, 1))
                act.activation(rows[:, 2 * TP:], m_args[:].rearrange("p a b -> p (a b)"), ACT.Exp)\
                    .then_inc(exps_ready.sem, 1)
                act.wait_ge(*args_ready.at(l, 2))
                act.activation(tmp[1][0:NH, 0:TP], tmp[1][0:NH, 0:TP], ACT.Exp).then_inc(exps_ready.sem, 1)
                act.wait_ge(*centered.at(l, 1))
                for j in range(2):
                    act.activation(tmp[2 + j][:], gv[:, j, :], ACT.Square).then_inc(c_square.sem, 1)
                for t in range(2):
                    act.wait_ge(*tok_done.at(l, t + 1))
                    act.activation(k_tok[:, 2 * t:2 * t + 2, :, :].rearrange("p a b c -> p a (b c)"), ps[t][:],
                                   ACT.Copy).then_inc(ktok_ready.sem, 1)
                act.wait_ge(*var_done.at(l, 1))
                act.activation(two(tmp[2][:]), ps[2][:, :, 0:HT], ACT.Sqrt, bias=LN_EPS, scale=1.0 / 256)\
                    .then_inc(var_root.sem, 1)
                act.wait_ge(*vnT_done.at(l, 1))
                act.activation(vn_tok[:].rearrange("p (b c) n -> p b (c n)", b=2), ps[2][:], ACT.Copy)\
                    .then_inc(vnT_ready.sem, 1)
                act.wait_ge(*pooled.at(l, 1))
                act.wait_ge(*gmlp_ready.at(l, 1))
                for j in range(2):
                    act.activation(two(gv[:, j, :]), ps[j][:, :, 0:HT], ACT.Copy,
                                   scale=vec[:, V_SPOOL + j:V_SPOOL + j + 1]).then_inc(pool_ready.sem, 1)
                for h in range(NH):
                    at = 0
                    for j in range(NC):
                        n = TP - j * P
                        act.wait_ge(*d_ready.at(l, h * NC + j + 1))
                        act.activation(sw[:, at:at + n], sw[:, at:at + n], ACT.Exp).then_inc(w_ready.sem, 1)
                        at += n
                    act.wait_ge(*head_sums.at(l, h + 1))
                    act.activation(tmp[0][:, 0:TP], ps[3][:, 1, :], ACT.Abs).then_inc(den_abs.sem, 1)
                act.wait_ge(*C_done.at(l, 1))
                own.mark(act.activation(C_out[:].rearrange("p a b -> p (a b)"), ps[0][:, 0, :], ACT.Copy))
                act.activation(n_out[:], ps[0][:, 1, 0:NH], ACT.Copy).then_inc(C_ready.sem, 1)
                act.wait_ge(*vrow_done.at(l, 1))
                act.activation(tmp[2][0:NS, 0:TP], ps[1][0:NS, 0, :], ACT.Copy).then_inc(vrow_ready.sem, 1)
                for b in range(NS):
                    act.wait_ge(*vb_done.at(l, b + 1))
                    if b >= 2:
                        act.wait_ge(*Cs_ready.at(l, b - 1))
                    for h in range(NH):
                        r = act.activation(tmp[b % 2][:, h * P:(h + 1) * P], ps[2][:, b % 2, h * P:(h + 1) * P],
                                           ACT.Copy, scale=kw_s[:, h, b:b + 1])
                        if h < NH - 1:
                            own.mark(r)
                    r.then_inc(vkw_ready.sem, 1)
                act.wait_ge(*num_done.at(l, 1))
                act.activation(den_s[:].rearrange("p a b -> p (a b)"), ps[3][:, 1, 0:NH * NS], ACT.Abs)\
                    .then_inc(dens_abs.sem, 1)
                act.wait_ge(*hs_ready.at(l, 1))
                act.activation(k[:], q[:], ACT.Square).then_inc(h_square.sem, 1)
                for h in range(NH):
                    act.wait_ge(*h_summed.at(l, h + 1))
                    act.activation(two(v[:, h, :]), ps[h][:, :, 0:HT], ACT.Sqrt, bias=EPS, scale=1.0 / P)\
                        .then_inc(h_root.sem, 1)
                act.activation(cat_h[:, 0:2, :], gv[:], ACT.Copy).then_inc(cat_hi.sem, 1)
                act.activation(cat_h[:, 6:8, :], gu[:], ACT.Copy).then_inc(cat_hi.sem, 1)
                act.wait_ge(*h_ready.at(l, 1))
                act.activation(cat_h[:, 2:6, :], q[:], ACT.Copy).then_inc(cat_hi.sem, 1)

            def branches(l):
                def evict(i, s):
                    for u in range(2):
                        g = 2 * s + u
                        act.wait_ge(*done("branch", l, i * 4 + (g + 1)))
                        if g < 3:
                            act.wait_ge(*branch_read.at(l, i * 5))
                            act.activation(two(tmp[g][:]), ps[g][:, :, 0:HT], ACT.Sigmoid)\
                                .then_inc(gate_ready.sem, 1)
                        else:
                            act.wait_ge(*branch_read.at(l, i * 5 + 5))
                            m = bass.ds(i, 1) if not isinstance(i, int) else slice(i, i + 1)
                            act.activation(mrg_h[:, m, :], tmp[3][:].unsqueeze(1), ACT.Copy).then_inc(mrg_hi.sem, 1)

                stream(l, "branch", 8, FULL, evict, FULL)

            def memory(l):
                act.wait_ge(mem_loaded.sem, l * 16 + 16)
                for m in range(KD):
                    act.wait_ge(*x_summed.at(l, PRE_MEM * KD + max(m - 1, 0)))
                    act.activation(tmp[2 + m % 2][:, 0:M], mem[:, m, :], ACT.Square).then_inc(x_square.sem, 1)
                act.wait_ge(*x_summed.at(l, (PRE_MEM + 1) * KD))
                act.activation(rms[:, 0:M], ps[1][:, 0, 0:M], ACT.Sqrt, bias=EPS, scale=1.0 / D)\
                    .then_inc(root_ready.sem, 1)
                for m in range(KD):
                    act.wait_ge(*xn_ready.at(l, PRE_MEM * KD + m + 1))
                    act.activation(mem_h[:, m, :], tmp[m % 2][:, 0:M], ACT.Copy).then_inc(xh_ready.sem, 1)

                def tile(dst, i, n):
                    return dst[:, bass.ds(n, 1), :] if not isinstance(i, int) else dst[:, n:n + 1, :]

                def evict_k(i, s):
                    for u in range(2):
                        act.wait_ge(*done("mk", l, i * 4 + (2 * s + u + 1)))
                        act.activation(tile(mk, i, i * 4 + (2 * s + u)), ps[2 * s + u][:, 0:1, 0:M], ACT.Copy)\
                            .then_inc(kv_first.sem if u == 0 else pair_evicted[s].sem, 1)

                def evict_v(i, s):
                    for u in range(2):
                        act.wait_ge(*done("mv", l, i * 4 + (2 * s + u + 1)))
                        act.activation(tile(mvT, i, i * 4 + (2 * s + u)), ps[2 * s + u][:, 0:1, 0:M], ACT.Copy)\
                            .then_inc(kv_first.sem if u == 0 else pair_evicted[s].sem, 1)

                stream(l, "mk", 2, FULL, evict_k, FULL)
                stream(l, "mv", 2, FULL, evict_v, FULL)

                def evict_q(i, s):
                    for u in range(2):
                        act.wait_ge(*done("mq", l, i * 4 + (2 * s + u + 1)))
                        n = i * 4 + (2 * s + u)
                        dst = qm[:, n, :] if isinstance(i, int) else \
                            qm[:, bass.ds(n, 1), :].rearrange("p a t -> p (a t)")
                        act.activation(two(dst), ps[2 * s + u][:, :, 0:HT], ACT.Copy, scale=float(M) ** -0.5)\
                            .then_inc(q_first.sem if u == 0 else pair_evicted[s].sem, 1)

                stream(l, "mq", 2, FULL, evict_q, FULL)

            def attention(l):
                def exps(h):
                    act.wait_ge(*max_ready.at(l, h + 1))
                    act.wait_ge(*(pT_done.at(l, h) if h else mvT_done.at(l, 1)))
                    for t in range(NC):
                        r = act.activation(prob[:, t, :], ps[h % 2][:, t // 2, (t % 2) * M:(t % 2 + 1) * M],
                                           ACT.Exp, bias=att_max[:, h % 2, t:t + 1], accum_out=att_sum[:, t:t + 1])
                        if t < NC - 1:
                            own.mark(r)
                    r.then_inc(p_ready.sem, 1)

                def transposed(h):
                    act.wait_ge(*pT_done.at(l, h + 1))
                    act.activation(probT[:], ps[2][:], ACT.Copy).then_inc(pT_ready.sem, 1)

                def output(h):
                    act.wait_ge(*o_done.at(l, h + 1))
                    act.activation(xh[:, 2 * h:2 * h + 2, 0:TP], ps[h % 2][:], ACT.Copy).then_inc(oh_ready.sem, 1)

                exps(0)
                for h in range(NH):
                    transposed(h)
                    if h + 1 < NH:
                        exps(h + 1)
                    output(h)
                    if h == 2:
                        act.wait_ge(*smax_ready.at(l, 1))
                        for g in range(NH):
                            r = act.activation(prob_s[:, g, :], ps[3][0:NS, g // 2, (g % 2) * M:(g % 2 + 1) * M],
                                               ACT.Exp, bias=att_smax[:, g:g + 1], accum_out=att_ssum[:, g:g + 1])
                            if g < NH - 1:
                                own.mark(r)
                        r.then_inc(sexp_ready.sem, 1)
                act.wait_ge(*v_used.at(l, NS))
                act.activation(o_rows[:].rearrange("p (a b) -> p a b", a=2), ps[3][0:NS, :, :], ACT.Copy)\
                    .then_inc(orow_ready.sem, 1)
                act.wait_ge(*oT_done.at(l, 1))
                act.activation(xh[:, :, TP:T], ps[2][:, 0, 0:64].rearrange("p (a b) -> p a b", a=KD), ACT.Copy)\
                    .then_inc(oh_ready.sem, 1)

            with act.Fori(0, L) as l:
                own.begin(l)
                hi(l, TURNS["up_a"], 0, FULL)
                pre(l, PRE_A, 0)
                ffn(l, 0, "up_a", "down_a", FULL)
                post(l, 0)
                pre(l, PRE_MIX, 1)
                evict = evict_in(l)
                for i in range(6):
                    hi(l, TURNS["in"] + i, 1, FULL)
                    evict(i, 0)
                    hi(l, TURNS["in"] + i + 1, 0, FULL)
                    evict(i, 1)
                mixer(l)
                branches(l)
                stream(l, "out", 2, FULL, squares(l, 1, "out"), FULL)
                post(l, 1)
                pre(l, PRE_ATT, 2)
                memory(l)
                attention(l)
                stream(l, "mo", 2, FULL, squares(l, 2, "mo"), FULL)
                post(l, 2)
                pre(l, PRE_B, 3)
                act.wait_ge(out_mem.sem, l * 32 + 32)
                ffn(l, 1, "up_b", "down_b", None)
                post(l, 3)
                own.end("scalar")

        @block.vector
        def _(dve):
            own = Steps(dve, vector_step)
            dve.memset(zeros8[:], 0.0).then_inc(zeros_ready.sem, 1)
            dve.sem_inc(pair_evicted[0].sem, 1)
            dve.sem_inc(pair_evicted[1].sem, 1)
            dve.sem_inc(hidden_lo.sem, hidden_lo.credit)
            dve.sem_inc(y_summed.sem, y_summed.credit)
            dve.sem_inc(branch_read.sem, branch_read.credit)
            dve.wait_ge(s_x.sem, 8 * 16)
            for n, g in enumerate((gain(0, 1), gain(3, 1))):
                dve.tensor_scalar(vec_all[:, :, g:g + KD], vec_all[:, :, g:g + KD], 0.5, None, ALU.mult)\
                    .then_inc(const_scaled.sem, 1)
            dve.wait_ge(const_scaled.sem, 2)

            def start_sum(l, group):
                dve.memset(ssq[:], 0.0).then_inc(y_summed.sem, 1)

            def evict_y(l, group, units_at, m, tile, last):
                dve.wait_ge(*y_square.at(l, m + (group * KD + 1)))
                dve.wait_ge(*y_summed.at(l, m + (group * (KD + 1) + 1)))
                dve.tensor_tensor(ssq[:], ssq[:], tmp[tile % 2 if units_at else tile // 2][:], ALU.add)\
                    .then_inc(y_summed.sem, 1)
                dst = y[:, m, :] if isinstance(m, int) else y[:, bass.ds(m, 1), :].rearrange("p a t -> p (a t)")
                dve.tensor_copy(two(dst), ps[tile][:, :, 0:HT]).then_inc(last.sem, 1)

            def linear_y(l, group, phase):
                start_sum(l, group)
                with dve.Fori(0, 2) as i:
                    for s in range(2):
                        for u in range(2):
                            evict_y(l, group, True, i * 4 + (2 * s + u), 2 * s + u,
                                    y_copied if u == 0 else pair_evicted[s])

            def ffn(l, n, up, down):
                with dve.Fori(0, 11) as i:
                    for s in range(2):
                        f = i * 2 + s
                        at = f + n * KF
                        dve.wait_ge(*silu_ready.at(l, at + 1))
                        dve.wait_ge(*done(up, l, i * 4 + (2 * s + 2)))
                        dve.wait_ge(*hidden_lo.at(l, at - 1))
                        dve.tensor_tensor(two(tmp[2 + s][:]), two(tmp[s][:]), ps[2 * s + 1][:, :, 0:HT], ALU.mult)\
                            .then_inc(pair_evicted[s].sem, 1)
                        dve.wait_ge(*hidden_hi.at(l, at + 1))
                        dve.tensor_tensor(hid_l[:, bass.ds(f, 1), :], tmp[2 + s][:].unsqueeze(1),
                                          hid_h[:, bass.ds(f, 1), :].bitcast(F32), ALU.subtract)\
                            .then_inc(hidden_lo.sem, 1)
                start_sum(l, 3 * n)
                with dve.Fori(0, 4) as i:
                    for mm in range(2):
                        evict_y(l, 3 * n, False, i * 2 + mm, 2 * mm, pair_evicted[mm])

            def post(l, n, g):
                dve.wait_ge(*root_ready.at(l, ROOT_POST[n] + 1))
                own.link(dve.reciprocal(rms[:], rms[:]))

                def scaled(m):
                    if m >= 2:
                        dve.wait_ge(*x_updated.at(l, n * KD + m - 1))
                    own.mark(dve.scalar_tensor_tensor(out=tmp[m % 2][:], in0=y[:, m, :], scalar=vec[:, g + m:g + m + 1],
                                                      in1=rms[:], op0=ALU.mult, op1=ALU.mult))
                    return own.n

                nxt = scaled(0)
                for m in range(KD):
                    mine = nxt
                    if m + 1 < KD:
                        nxt = scaled(m + 1)
                    dve.wait_ge(*vector_step.at(l, mine))
                    dve.tensor_tensor(x[:, m, :], x[:, m, :], tmp[m % 2][:], ALU.add).then_inc(x_updated.sem, 1)

            def pre(l, n, g, src, n_tok, dst_h, dst_l):
                dve.wait_ge(*root_ready.at(l, ROOT_PRE[n] + 1))
                own.link(dve.reciprocal(rms[:, 0:n_tok], rms[:, 0:n_tok]))

                def normal(m):
                    if m >= 2:
                        dve.wait_ge(*xl_ready.at(l, n * KD + m - 1))
                    dve.scalar_tensor_tensor(out=tmp[m % 2][:, 0:n_tok], in0=src[:, m, :],
                                             scalar=vec[:, g + m:g + m + 1], in1=rms[:, 0:n_tok],
                                             op0=ALU.mult, op1=ALU.mult).then_inc(xn_ready.sem, 1)

                normal(0)
                for m in range(KD):
                    if m + 1 < KD:
                        normal(m + 1)
                    dve.wait_ge(*xh_ready.at(l, n * KD + m + 1))
                    dve.tensor_tensor(dst_l[:, m, :], tmp[m % 2][:, 0:n_tok], dst_h[:, m, :].bitcast(F32),
                                      ALU.subtract).then_inc(xl_ready.sem, 1)

            def gates_rows(l):
                dve.wait_ge(*done("in", l, 23))
                own.mark(dve.tensor_scalar(two(tmp[0][0:NH, :]), ps[2][0:NH, :, 0:HT], vec[0:NH, V_BI:V_BI + 1],
                                           None, ALU.add))
                dve.wait_ge(*done("in", l, 24))
                dve.tensor_scalar(two(tmp[1][0:NH, :]), ps[3][0:NH, :, 0:HT], vec[0:NH, V_BF:V_BF + 1],
                                  None, ALU.add).then_inc(pair_evicted[1].sem, 1)

            def mixer(l):
                ig, lf, sp_, mt = (tmp[n][0:NH, :] for n in range(4))
                one, a, g = ssq[0:NH, 0:TP], rms[0:NH, 0:TP], ssq[0:NH, 0:TP]
                dve.memset(pin[:, :, 0:PAD], 0.0).then_inc(win_zero.sem, 1)
                dve.wait_ge(*evicted("in", 0, l, 1))
                own.mark(dve.tensor_copy(pool_last[:], pin[:, :, PAD + TP - 15:PAD + TP]))
                own.mark(dve.tensor_copy(pool_new[:, :, :, 14:15], pin[:, :, PAD + TP:].unsqueeze(3)))
                gates_rows(l)
                own.mark(dve.memset(one, 1.0))
                dve.wait_ge(*softplus_ready.at(l, 1))
                own.link(dve.scalar_tensor_tensor(out=lf, in0=lf, scalar=0.0, in1=sp_, op0=ALU.min, op1=ALU.subtract))
                own.link(dve.tensor_tensor_scan(mt[:, 0:TP], one, lf[:, 0:TP], 0.0, ALU.mult, ALU.add))
                own.link(dve.tensor_tensor(a, ig[:, 0:TP], mt[:, 0:TP], ALU.subtract))
                own.link(dve.tensor_tensor_scan(g, a, a, 0.0, ALU.max, ALU.max))
                dve.tensor_tensor(mt[:, 0:TP], mt[:, 0:TP], g, ALU.add).then_inc(mt_ready.sem, 1)
                own.link(dve.tensor_scalar(rows[:, 0:TP], g, -1.0, None, ALU.mult))
                own.mark(dve.tensor_copy(m_last[:], mt[:, TP - 1:TP]))
                dve.wait_ge(mix_loaded.sem, l * 96 + 96)
                own.mark(dve.tensor_copy(pool_new[:, :, :, 0:14], pool_state[:, :, :, 1:15]))
                own.link(dve.tensor_tensor(m_args[:, 0, :], lf[:, TP:T], m_state[:], ALU.add))
                own.link(dve.tensor_tensor(m_new[:], m_args[:, 0, :], ig[:, TP:T], ALU.max))
                own.mark(dve.tensor_tensor(m_args[:, 0, :], m_args[:, 0, :], m_new[:], ALU.subtract))
                own.mark(dve.tensor_tensor(m_args[:, 1, :], ig[:, TP:T], m_new[:], ALU.subtract))
                dve.tensor_scalar(m_args[:, 2, :], m_new[:], -1.0, None, ALU.mult).then_inc(args_ready.sem, 1)
                dve.tensor_scalar(lf[:, 0:TP], a, rows[:, TP - 1:TP], None, ALU.add).then_inc(args_ready.sem, 1)
                dve.wait_ge(*mean_done.at(l, 1))
                own.mark(dve.scalar_tensor_tensor(out=two(gv[:, 0, :]), in0=ps[2][:, :, 0:HT], scalar=-1.0 / 256,
                                                  in1=two(gv[:, 0, :]), op0=ALU.mult, op1=ALU.add))
                dve.wait_ge(*exps_ready.at(l, 3))
                dve.scalar_tensor_tensor(out=two(gv[:, 1, :]), in0=ps[2][:, :, 0:HT], scalar=-1.0 / 256,
                                         in1=two(gv[:, 1, :]), op0=ALU.mult, op1=ALU.add).then_inc(centered.sem, 1)
                dve.wait_ge(*cols_done.at(l, 1))
                dve.tensor_copy(cols[:].rearrange("p a b c -> p (a b c)"), ps[3][:, 0, 0:32])\
                    .then_inc(cols_ready.sem, 1)
                dve.tensor_copy(s_rows[:].rearrange("p a b c -> p (a b c)"), ps[3][:, 1, 0:96])\
                    .then_inc(cols_ready.sem, 1)
                dve.wait_ge(*var_root.at(l, 1))
                own.link(dve.reciprocal(tmp[2][:], tmp[2][:]))
                for j in range(2):
                    own.mark(dve.scalar_tensor_tensor(out=gv[:, j, :], in0=gv[:, j, :],
                                                      scalar=vec[:, V_LNG + j:V_LNG + j + 1], in1=tmp[2][:],
                                                      op0=ALU.mult, op1=ALU.mult))
                own.settle()
                for j in range(2):
                    own.mark(dve.tensor_scalar(gv[:, j, :], gv[:, j, :], vec[:, V_LNB + j:V_LNB + j + 1], None, ALU.add))
                own.settle()
                dve.tensor_copy(gv_out[:], gv[:, :, TP:T]).then_inc(vn_ready.sem, 1)
                for t in range(2):
                    dve.wait_ge(*tok_done.at(l, 3 + t))
                    dve.tensor_copy(v_tok[:, 2 * t:2 * t + 2, :, :].rearrange("p a b c -> p a (b c)"), ps[t][:])\
                        .then_inc(vtok_ready.sem, 1)
                dve.wait_ge(*win_ready.at(l, 4))
                groups = ((2, 0, 0, winA), (4, 0, 64, winB), (8, 1, 0, winA), (16, 1, 64, winB))
                for w, j, p0, win in groups:
                    r = slice(p0, p0 + 64)
                    own.mark(dve.tensor_tensor(win[r, j, PAD:2 * PAD], win[r, j, PAD:2 * PAD], early[r, j, :], ALU.mult))
                    own.mark(dve.tensor_reduce(pool_red[r, j, :], pool_state[r, j, :, 16 - w:15], AX.X, ALU.add))
                own.settle()
                for w, j, p0, win in groups:
                    r = slice(p0, p0 + 64)
                    own.mark(dve.scalar_tensor_tensor(out=winA[r, j, PAD:PAD + TP], in0=win[r, j, PAD:PAD + TP],
                                                      scalar=1.0 / w, in1=pin[r, j, PAD:PAD + TP],
                                                      op0=ALU.mult, op1=ALU.subtract))
                    own.mark(dve.tensor_tensor(pool_red[r, j, :], pool_red[r, j, :], pin[r, j, PAD + TP:], ALU.add))
                own.settle()
                for n, (w, j, p0, win) in enumerate(groups):
                    r = slice(p0, p0 + 64)
                    ins = dve.scalar_tensor_tensor(out=winA[r, j, PAD + TP:], in0=pool_red[r, j, :], scalar=1.0 / w,
                                                   in1=pin[r, j, PAD + TP:], op0=ALU.mult, op1=ALU.subtract)
                    if n < 3:
                        own.mark(ins)
                ins.then_inc(diff_ready.sem, 1)
                dve.wait_ge(*mixed_done.at(l, 1))
                for j in range(2):
                    own.mark(dve.tensor_tensor(tmp[j][:, 0:TP].rearrange("p (c t) -> p c t", c=NC),
                                               ps[3][:, j, :].rearrange("p (c t) -> p c t", c=NC),
                                               bs_m[:, j:j + 1, :].to_broadcast([P, NC, P]), ALU.add))
                    own.mark(dve.tensor_scalar(tmp[j][:, TP:T], gv[:, j, TP:T], vec[:, V_WS0 + j:V_WS0 + j + 1],
                                               vec[:, V_BS0 + j:V_BS0 + j + 1], ALU.mult, ALU.add))
                own.settle()
                own.mark(dve.tensor_tensor(gu[:, 0, :], gu[:, 0, :], tmp[0][:], ALU.mult))
                dve.tensor_tensor(gu[:, 1, :], gu[:, 1, :], tmp[1][:], ALU.mult).then_inc(gmlp_ready.sem, 1)
                for h in range(NH):
                    dve.wait_ge(*head_scores.at(l, h + 1))
                    if h:
                        dve.wait_ge(*head_sums.at(l, h))
                    at = 0
                    for j in range(NC):
                        n = TP - j * P
                        col = cols[:, 0, j, h:h + 1]
                        d = dve.scalar_tensor_tensor(out=sw[:, at:at + P], in0=ps[2][:, 0, j * P:(j + 1) * P],
                                                     scalar=col, in1=neg_mask[:], op0=ALU.add, op1=ALU.min)
                        if n > P:
                            own.mark(d)
                            d = dve.tensor_scalar(sw[:, at + P:at + n], ps[2][:, 0, (j + 1) * P:TP], col, 0.0,
                                                  ALU.add, ALU.min)
                        d.then_inc(d_ready.sem, 1)
                        at += n
                    at = 0
                    for j in range(NC):
                        n = TP - j * P
                        dve.wait_ge(*w_ready.at(l, h * NC + j + 1))
                        dve.tensor_tensor(sw[:, at:at + n], sw[:, at:at + n], ps[j // 2][:, j % 2, 0:n], ALU.mult)\
                            .then_inc(sw_ready.sem, 1)
                        at += n
                    dve.wait_ge(*den_abs.at(l, h + 1))
                    own.link(dve.tensor_tensor(tmp[1][:, 0:TP], tmp[0][:, 0:TP], ps[2][:, 1, :], ALU.max))
                    own.link(dve.reciprocal(tmp[1][:, 0:TP], tmp[1][:, 0:TP]))
                    dve.tensor_tensor(q[:, h, 0:TP], ps[3][:, 0, :], tmp[1][:, 0:TP], ALU.mult)\
                        .then_inc(head_ready.sem, 1)
                for h in range(NH):
                    for j in range(NC):
                        ins = dve.tensor_scalar(k_tok[:, h, j, :], k_tok[:, h, j, :], cols[:, 1, j, h:h + 1], None,
                                                ALU.mult)
                        if h * NC + j < NH * NC - 1:
                            own.mark(ins)
                ins.then_inc(kw_ready.sem, 1)
                own.link(dve.tensor_tensor(kw_s[:], k[:, :, TP:T], s_rows[:, :, 1, :], ALU.mult))
                own.link(dve.tensor_tensor(n_state[:], n_state[:], s_rows[:, :, 0, :], ALU.mult))
                own.link(dve.tensor_tensor(n_state[:], n_state[:], kw_s[:], ALU.add))
                dve.tensor_tensor(qn_s[:], n_state[:], q[:, :, TP:T], ALU.mult).then_inc(qn_ready.sem, 1)
                dve.wait_ge(C_loaded.sem, l * 16 + 16)
                for b in range(NS):
                    dve.wait_ge(*vkw_ready.at(l, b + 1))
                    for h in range(NH):
                        ins = dve.scalar_tensor_tensor(out=C_s[:, b, h, :], in0=C_s[:, b, h, :],
                                                       scalar=s_rows[:, h, 0, b:b + 1],
                                                       in1=tmp[b % 2][:, h * P:(h + 1) * P],
                                                       op0=ALU.mult, op1=ALU.add)
                        if h < NH - 1:
                            own.mark(ins)
                    ins.then_inc(Cs_ready.sem, 1)
                dve.wait_ge(*dens_abs.at(l, 1))
                own.link(dve.tensor_tensor(den_s[:], den_s[:], s_rows[:, :, 2, :], ALU.max))
                own.link(dve.reciprocal(den_s[:], den_s[:]))
                dve.tensor_tensor(q[:, :, TP:T], ps[3][:, 0, 0:NH * NS].rearrange("p (a b) -> p a b", a=NH), den_s[:],
                                  ALU.mult).then_inc(hs_ready.sem, 1)
                for h in range(NH):
                    dve.wait_ge(*h_root.at(l, h + 1))
                    own.link(dve.reciprocal(v[:, h, :], v[:, h, :]))
                    own.link(dve.scalar_tensor_tensor(out=q[:, h, :], in0=q[:, h, :],
                                                      scalar=vec[:, V_MLSTM + h:V_MLSTM + h + 1], in1=v[:, h, :],
                                                      op0=ALU.mult, op1=ALU.mult))
                    ins = dve.tensor_tensor(q[:, h, :], q[:, h, :], og[:, h, :], ALU.mult)
                    if h < NH - 1:
                        own.mark(ins)
                ins.then_inc(h_ready.sem, 1)
                for n, (lo_, hi_, src) in enumerate(((0, 2, gv), (6, 8, gu), (2, 6, q))):
                    dve.wait_ge(*cat_hi.at(l, n + 1))
                    dve.tensor_tensor(cat_l[:, lo_:hi_, :], src[:], cat_h[:, lo_:hi_, :].bitcast(F32), ALU.subtract)\
                        .then_inc(cat_lo.sem, 1)

            def branches(l):
                with dve.Fori(0, KD) as m:
                    for n in range(2):
                        dve.wait_ge(*gate_ready.at(l, m * 3 + (2 + n)))
                        dve.wait_ge(*branch_done.at(l, m * 2 + (n + 1)))
                        dve.tensor_tensor(two(tmp[1 + n][:]), two(tmp[1 + n][:]), ps[n][:, :, 0:HT], ALU.mult)\
                            .then_inc(branch_read.sem, 1)
                    dve.wait_ge(*done("branch", l, m * 4 + 4))
                    dve.tensor_tensor(two(tmp[0][:]), two(tmp[0][:]), ps[3][:, :, 0:HT], ALU.mult)\
                        .then_inc(branch_read.sem, 1)
                    dve.wait_ge(*branch_read.at(l, m * 5 + 3))
                    dve.tensor_tensor(tmp[1][:], tmp[1][:], tmp[2][:], ALU.add).then_inc(branch_read.sem, 1)
                    dve.wait_ge(*branch_read.at(l, m * 5 + 4))
                    dve.tensor_tensor(tmp[3][:], tmp[0][:], tmp[1][:], ALU.add).then_inc(branch_read.sem, 1)
                    dve.wait_ge(*mrg_hi.at(l, m + 1))
                    dve.tensor_tensor(mrg_l[:, bass.ds(m, 1), :], tmp[3][:].unsqueeze(1),
                                      mrg_h[:, bass.ds(m, 1), :].bitcast(F32), ALU.subtract).then_inc(mrg_lo.sem, 1)

            def attention(l):
                def maxima(h):
                    dve.wait_ge(*sc_done.at(l, h + 1))
                    dve.tensor_reduce(att_max[:, h % 2, :], ps[h % 2][:].rearrange("p b (t m) -> p (b t) m", t=2),
                                      AX.X, ALU.max, negate=True).then_inc(max_ready.sem, 1)

                def probs(h):
                    dve.wait_ge(*p_ready.at(l, h + 1))
                    own.link(dve.reciprocal(att_sum[:], att_sum[:]))
                    for t in range(NC):
                        ins = dve.tensor_scalar(prob[:, t, :], prob[:, t, :], att_sum[:, t:t + 1], None, ALU.mult)
                        if t < NC - 1:
                            own.mark(ins)
                    ins.then_inc(pn_ready.sem, 1)

                def lo_out(h):
                    dve.wait_ge(*oh_ready.at(l, h + 1))
                    dve.tensor_tensor(xl[:, 2 * h:2 * h + 2, 0:TP], ps[h % 2][:],
                                      xh[:, 2 * h:2 * h + 2, 0:TP].bitcast(F32), ALU.subtract)\
                        .then_inc(ol_ready.sem, 1)

                every = [P, KD, NS, NS]
                for s in range(2):
                    dve.wait_ge(*evicted("mq", s, l, 2))
                dve.tensor_tensor(q_one[:], qm[:, :, TP:T].unsqueeze(2).to_broadcast(every),
                                  eye8[:].unsqueeze(1).to_broadcast(every), ALU.mult).then_inc(q_one_ready.sem, 1)
                maxima(0)
                dve.wait_ge(*mvT_done.at(l, 1))
                for mt in range(2):
                    ins = dve.tensor_copy(mv[:, mt, :].rearrange("p (b n) -> p b n", b=2), ps[2 + mt][:])
                    if mt == 0:
                        own.mark(ins)
                ins.then_inc(mv_ready.sem, 1)
                maxima(1)
                probs(0)
                probs(1)
                for h in range(2):
                    lo_out(h)
                    maxima(h + 2)
                    probs(h + 2)
                lo_out(2)
                dve.wait_ge(*k_used.at(l, NS))
                dve.tensor_reduce(att_smax[:], ps[3][0:NS].rearrange("p b (t m) -> p (b t) m", t=2), AX.X, ALU.max,
                                  negate=True).then_inc(smax_ready.sem, 1)
                dve.wait_ge(*sexp_ready.at(l, 1))
                own.link(dve.reciprocal(att_ssum[:], att_ssum[:]))
                for h in range(NH):
                    ins = dve.tensor_scalar(prob_s[:, h, :], prob_s[:, h, :], att_ssum[:, h:h + 1], None, ALU.mult)
                    if h < NH - 1:
                        own.mark(ins)
                ins.then_inc(sp_ready.sem, 1)
                dve.wait_ge(*spT_done.at(l, 1))
                dve.tensor_tensor(p_one[:], ps[3][:, 0, 0:KD * NS].rearrange("p (f s) -> p f s", f=KD).unsqueeze(2)
                                  .to_broadcast(every), eye8[:].unsqueeze(1).to_broadcast(every), ALU.mult)\
                    .then_inc(spT_ready.sem, 1)
                lo_out(3)
                dve.wait_ge(*oh_ready.at(l, NH + 1))
                dve.tensor_tensor(xl[:, :, TP:T], ps[2][:, 0, 0:64].rearrange("p (a b) -> p a b", a=KD),
                                  xh[:, :, TP:T].bitcast(F32), ALU.subtract).then_inc(ol_ready.sem, 1)

            with dve.Fori(0, L) as l:
                own.begin(l)
                dve.tensor_copy(vec[:], vec_all[:, bass.ds(l, 1), :].rearrange("p a n -> p (a n)"))\
                    .then_inc(vec_ready.sem, 1)
                dve.wait_ge(*vec_ready.at(l, 1))
                pre(l, PRE_A, gain(0, 0), x, T, xh, xl)
                ffn(l, 0, "up_a", "down_a")
                post(l, 0, gain(0, 1))
                pre(l, PRE_MIX, gain(1, 0), x, T, xh, xl)
                mixer(l)
                branches(l)
                linear_y(l, 1, "out")
                post(l, 1, gain(1, 1))
                pre(l, PRE_ATT, gain(2, 0), x, T, xh, xl)
                pre(l, PRE_MEM, V_MEM, mem, M, mem_h, mem_l)
                attention(l)
                linear_y(l, 2, "mo")
                post(l, 2, gain(2, 1))
                pre(l, PRE_B, gain(3, 0), x, T, xh, xl)
                ffn(l, 1, "up_b", "down_b")
                post(l, 3, gain(3, 1))
                own.end("vector")


def _layout(inp):
    f = np.float32
    cut = np.ascontiguousarray
    a = {k: np.asarray(v) for k, v in inp.items()}

    def tiles(w):
        K, N = w.shape
        return w.reshape(K // P, P, N // P, P).transpose(2, 1, 0, 3)

    def cols(w):
        return w.reshape(-1, P).T

    x = np.concatenate([a["x_prompt"][0], a["x_sample"][:, 0]], axis=0)
    out = {"xT": cut(x.T.reshape(KD, P, T).transpose(1, 0, 2)),
           "memT": cut(a["mem_prompt"][0].T.reshape(KD, P, M).transpose(1, 0, 2))}
    full, down, vecs = [], [], []
    for l in range(L):
        w_in = a["w_in"][l]
        up = [tiles(a["w_ff_in"][l, n]) for n in range(2)]
        ups = [np.stack([u[:KF], u[KF:]], axis=1).reshape(2 * KF, P, KD, P) for u in up]
        first = tiles(w_in[:, :2304])
        i_f = np.stack([w_in[:, c:c + P].reshape(KD, P, P).transpose(1, 0, 2) for c in (2304, 2308)])
        ugv = tiles(w_in[:, 2312:2824])
        gates = tiles(w_in[:, 2824:]).reshape(3, KD, P, KD, P)
        br = tiles(np.concatenate([a["w_br_pool"][l], a["w_br_mlstm"][l], a["w_br_gmlp"][l]], axis=0))
        branch = np.stack([gates[0], gates[1], gates[2], br], axis=1).reshape(4 * KD, P, KD, P)
        units = [ups[0], first, ugv, i_f, branch] + [tiles(a[n][l]) for n in ("w_out", "w_mk", "w_mv", "w_mq", "w_mo")]
        units = np.concatenate(units + [ups[1]], axis=0)
        full.append(units.reshape(FULL_PAIRS, 2, P, KD * P).transpose(0, 2, 1, 3).reshape(FULL_PAIRS, P, 2 * KD * P))
        for n in range(2):
            w = tiles(a["w_ff_out"][l, n])
            down.append(w.reshape(KD, P, 2, 11 * P).transpose(0, 2, 1, 3).reshape(2 * KD, P, 11 * P))
        ws0, bs0 = a["w_s"][l, :, 0, 0], a["b_s"][l, :, 0]
        b_i, b_f = np.zeros((P, 1), f), np.zeros((P, 1), f)
        b_i[:NH, 0], b_f[:NH, 0] = a["b_igate"][l], a["b_fgate"][l]
        vecs.append(np.concatenate(
            [cols(a["norm_g"][l].reshape(-1)), cols(a["g_mem"][l]), cols(a["g_mlstm"][l]), cols(a["gmlp_ln_g"][l]),
             cols(a["gmlp_ln_b"][l]), cols(a["s_pool"][l]), cols(np.repeat(ws0, 64)), cols(np.repeat(bs0, 64)),
             b_i, b_f], axis=1))
    out["w_full"] = cut(np.concatenate(full, axis=0))
    out["w_down"] = cut(np.concatenate(down, axis=0))
    out["vecs"] = cut(np.stack(vecs, axis=1))
    wp = np.zeros((L, P, 2, P), f)
    for g in range(4):
        r = slice(64 * (g % 2), 64 * (g % 2) + 64)
        wp[:, r, g // 2, r] = a["w_pool"][:, g]
    out["wpool"] = wp.reshape(L, P, 2 * P)
    out["wsT"] = cut(a["w_s"].transpose(0, 3, 1, 2).reshape(L, P, 4 * P))
    out["bsT"] = cut(np.repeat(a["b_s"].reshape(L, 2, 2, 1, P), 64, axis=3).transpose(0, 2, 3, 1, 4).reshape(L, P, 2 * P))
    out["poolT"] = cut(a["state_pool"].transpose(0, 3, 1, 2).reshape(L, 2, P, NS * 15).transpose(0, 2, 1, 3)
                       .reshape(L, P, 2 * NS * 15))
    out["CT"] = cut(a["state_mlstm_C"].transpose(0, 4, 1, 2, 3).reshape(L, P, NS * NH * P))
    out["nT"] = cut(a["state_mlstm_n"].transpose(0, 3, 2, 1).reshape(L, P, NH * NS))
    out["mT"] = cut(a["state_mlstm_m"].transpose(0, 2, 1))
    out["kT"] = cut(a["cache_mem_k"].transpose(0, 1, 3, 4, 2).reshape(L * NS, KD, P, M).transpose(0, 2, 1, 3)
                    .reshape(L * NS, P, KD * M))
    out["vC"] = cut(a["cache_mem_v"].reshape(L * NS, 2, P, D).transpose(0, 2, 1, 3).reshape(L * NS, P, 2 * D))
    s, t = np.arange(P)[:, None], np.arange(P)[None, :]
    window = np.repeat(np.array([[2, 8], [4, 16]]), 64, axis=0)[:, :, None]
    early = window / np.minimum(np.arange(PAD)[None, None, :] + 1, window)
    out["consts"] = np.concatenate([np.ones((P, P)), s == t, np.where(s <= t, 0.0, NEG), s <= t,
                                    early.reshape(P, 2 * PAD),
                                    np.broadcast_to(np.eye(NS).reshape(1, -1), (P, NS * NS))], axis=1).astype(f)
    return out


_OUTS = [("o_y", (P, KD, T)), ("o_pool_p", (L, P, 2 * 15)), ("o_pool_s", (L, P, 2 * NS * 15)), ("o_C", (L, P, NH * P)),
         ("o_n", (L, P, NH)), ("o_m", (L, NH, 1)), ("o_CT", (L, P, NS * NH * P)), ("o_nT", (L, P, NH * NS)),
         ("o_mT", (L, NH, NS)), ("o_mk", (L, P, KD * M)), ("o_mv", (L, P, 2 * D)), ("o_gv", (L, P, 2 * NS))]


def kernel(**inputs):
    import concourse.bacc as _bacc
    from concourse.bass_utils import run_bass_kernel_spmd as _run

    nc = _bacc.Bacc("TRN2", target_bir_lowering=False, num_devices=1)
    arrays = _layout(inputs)
    args = [nc.dram_tensor(n, a.shape, F32, kind="ExternalInput").ap() for n, a in arrays.items()]
    args += [nc.dram_tensor(n, shape, F32, kind="ExternalOutput").ap() for n, shape in _OUTS]
    build(nc, *args)
    r = _run(nc, [arrays], core_ids=[0]).results[0]
    y = r["o_y"].transpose(1, 0, 2).reshape(D, T).T
    pool_p = r["o_pool_p"].reshape(L, P, 2, 15).transpose(0, 3, 2, 1).reshape(L, 1, 15, 256)
    pool_s = r["o_pool_s"].reshape(L, P, 2, NS, 15).transpose(0, 3, 4, 2, 1).reshape(L, NS, 15, 256)
    C_p = r["o_C"].reshape(L, P, NH, P).transpose(0, 2, 1, 3)[:, None]
    n_p = r["o_n"].transpose(0, 2, 1)[:, None]
    m_p = r["o_m"].transpose(0, 2, 1)
    C_s = r["o_CT"].reshape(L, P, NS, NH, P).transpose(0, 2, 3, 4, 1)
    n_s = r["o_nT"].reshape(L, P, NH, NS).transpose(0, 3, 2, 1)
    m_s = r["o_mT"].transpose(0, 2, 1)
    mk = r["o_mk"].reshape(L, P, KD, M).transpose(0, 3, 2, 1).reshape(L, 1, M, NH, D // NH)
    mv = r["o_mv"].reshape(L, P, 2, D).transpose(0, 2, 1, 3).reshape(L, 1, M, NH, D // NH)
    gv = r["o_gv"].reshape(L, P, 2, NS).transpose(0, 3, 2, 1).reshape(L, NS, 1, 256)
    cut = np.ascontiguousarray
    return tuple(cut(t) for t in (y[None, :TP], y[TP:, None], pool_p, pool_s, C_p, n_p, m_p, C_s, n_s, m_s, mk, mv, gv))
```

```python
from contextlib import ExitStack

import numpy as np

import concourse.bass as bass
from concourse import mybir

ALU = mybir.AluOpType
ACT = mybir.ActivationFunctionType
AX = mybir.AxisListType
F32 = mybir.dt.float32
F32R = mybir.dt.float32r

P = 128
L = 2
D = 1024
KD = D // P
TP = 512
NS = 8
T = TP + NS
HT = T // 2
FF = 2816
KF = FF // P
NH = 4
NC = TP // P
M = 256
EPS = 1e-6
LN_EPS = 1e-5
PAD = 16
TPAD = PAD + T
NEG = -1e30

def gain(sub, post):
    return (2 * sub + post) * KD
V_MEM, V_MLSTM, V_LNG, V_LNB, V_SPOOL, V_WS0, V_BS0, V_BI, V_BF, NV = 64, 72, 76, 78, 80, 82, 84, 86, 87, 88

TURNS, _t = {}, 0
for _name, _n in (("up_a", 11), ("down_a", 8), ("in", 6), ("branch", 8), ("out", 2), ("mk", 2),
                  ("mv", 2), ("mq", 2), ("mo", 2), ("up_b", 11), ("down_b", 8)):
    TURNS[_name] = _t
    _t += _n
TURNS_LAYER = _t
UNITS_LAYER = 4 * TURNS_LAYER
FULL = ((8, 8), (8, 8))
DOWN = ((6, 5), (6, 5))
FULL_AT = {"up_a": 0, "in": 22, "branch": 34, "out": 50, "mk": 54, "mv": 58, "mq": 62, "mo": 66, "up_b": 70}
FULL_PAIRS = 92

EVICTED = {"up_a": 0, "down_a": 11, "in": 15, "out": 21, "mk": 23, "mv": 25, "mq": 27, "mo": 29, "up_b": 31,
           "down_b": 42}
EVICTED_LAYER = 46
PRE_A, PRE_MIX, PRE_ATT, PRE_B = range(4)
ROOT_PRE = (0, 2, 4, 6)
ROOT_POST = (1, 3, 5, 7)
SCALAR_STEPS, VECTOR_STEPS = 58, 132


class Signal:

    def __init__(self, sem, per_layer, credit=0):
        self.sem, self.per_layer, self.credit = sem, per_layer, credit

    def at(self, layer, n):
        return self.sem, layer * self.per_layer + (n + self.credit)


class Steps:

    def __init__(self, eng, signal):
        self.eng, self.steps, self.n, self.layer = eng, signal, 0, None

    def begin(self, layer):
        self.n, self.layer = 0, layer

    def link(self, ins):
        self.mark(ins)
        self.settle()

    def mark(self, ins):
        self.n += 1
        ins.then_inc(self.steps.sem, 1)

    def settle(self):
        self.eng.wait_ge(*self.steps.at(self.layer, self.n))

    def end(self, name):
        assert self.n == self.steps.per_layer, (name, self.n)


def build(nc, xT, memT, w_full, w_down, vecs, wpool, wsT, bsT, poolT, CT, nT, mT, kT, vC, consts,
          o_y, o_pool_p, o_pool_s, o_C, o_n, o_m, o_CT, o_nT, o_mT, o_mk, o_mv, o_gv):
    with ExitStack() as ctx:
        def sb(name, shape, dt=F32):
            return ctx.enter_context(nc.sbuf_tensor(name, shape, dt))

        def signal(name, per_layer=1, credit=0):
            return Signal(ctx.enter_context(nc.semaphore(name)), per_layer, credit)

        x = sb("x", [P, KD, T])
        xh = sb("xh", [P, KD, T], F32R)
        xl = sb("xl", [P, KD, T], F32R)
        w_raw = sb("w_raw", [P, 2, 2 * KD * P])
        w_hi = sb("w_hi", [P, 2, KD * P], F32R)
        w_lo = sb("w_lo", [P, 2, KD * P], F32R)
        tmp = [sb(f"tmp{n}", [P, T]) for n in range(4)]
        ssq = sb("ssq", [P, T])
        rms = sb("rms", [P, T])
        mem_rms = sb("mem_rms", [P, M])
        ones = sb("ones", [P, P])
        ident = sb("ident", [P, P])
        neg_mask = sb("neg_mask", [P, P])
        causal = sb("causal", [P, P])
        early = sb("early", [P, 2, PAD])
        vec_all = sb("vec_all", [P, L, NV])
        vec = sb("vec", [P, NV])
        pool_state = sb("pool_state", [P, 2, NS, 15])
        pool_red = sb("pool_red", [P, 2, NS])
        pool_last = sb("pool_last", [P, 2, 15])
        pool_new = sb("pool_new", [P, 2, NS, 15])
        n_state = sb("n_state", [P, NH, NS])
        m_state = sb("m_state", [NH, NS])
        m_new = sb("m_new", [NH, NS])
        m_last = sb("m_last", [NH, 1])
        m_args = sb("m_args", [NH, 3, NS])
        cols = sb("cols", [P, 3, NC, NH])
        s_rows = sb("s_rows", [P, NH, 3, NS])
        kw_s = sb("kw_s", [P, NH, NS])
        qn_s = sb("qn_s", [P, NH, NS])
        den_s = sb("den_s", [P, NH, NS])
        h_den = sb("h_den", [P, NH, NC])
        h_sum = sb("h_sum", [P, NH, NC])
        h_rms = sb("h_rms", [P, NH, NC])
        n_out = sb("n_out", [P, NH])
        gv_out = sb("gv_out", [P, 2, NS])
        eye8 = sb("eye8", [P, NS, NS])
        zeros8 = sb("zeros8", [P, NS])
        att_max = sb("att_max", [P, 2, NC])
        att_sum = sb("att_sum", [P, NC])
        att_smax = sb("att_smax", [NS, NH])
        att_ssum = sb("att_ssum", [NS, NH])

        arena = sb("arena", [P, 2 * KF * T])
        y_arena = sb("y_arena", [P, KD * T])
        arena_at, y_at = nc.lookup_mloc(arena).addr, nc.lookup_mloc(y_arena).addr

        def view(name, shape, offset, dt=F32, base=None):
            size = int(np.prod(shape[1:])) * 4
            assert offset + size <= (2 * KF * T * 4 if base is None else KD * T * 4), name
            return nc.alloc_sbuf_tensor_at(name, shape, dt, offset=(arena_at if base is None else base) + offset)

        BT = KD * T * 4
        hid_h = view("hid_h", [P, KF, T], 0, F32R)
        hid_l = view("hid_l", [P, KF, T], KF * T * 4, F32R)
        y = view("y", [P, KD, T], 0, base=y_at)
        cat_h = view("cat_h", [P, KD, T], 0, F32R)
        cat_l = view("cat_l", [P, KD, T], BT, F32R)
        mrg_h = view("mrg_h", [P, KD, T], 2 * BT, F32R)
        mrg_l = view("mrg_l", [P, KD, T], 3 * BT, F32R)
        k_tok = view("k_tok", [P, NH, NC, P], 0)
        v_tok = view("v_tok", [P, NH, NC, P + 1], NH * TP * 4)
        at = BT
        vn_tok = view("vn_tok", [P, NC, 256], at); at += NC * 256 * 4
        winA = view("winA", [P, 2, TPAD], at); at += 2 * TPAD * 4
        winB = view("winB", [P, 2, TPAD], at); at += 2 * TPAD * 4
        ws_m = view("ws_m", [P, 4, P], at); at += 4 * P * 4
        bs_m = view("bs_m", [P, 2, P], at)
        at += 2 * P * 4
        assert at <= 2 * BT
        at = 2 * BT
        q = view("q", [P, NH, T], at); at += NH * T * 4
        k = view("k", [P, NH, T], at); at += NH * T * 4
        v = view("v", [P, NH, T], at); at += NH * T * 4
        og = view("og", [P, NH, T], at); at += NH * T * 4
        gu = view("gu", [P, 2, T], at); at += 2 * T * 4
        gv = view("gv", [P, 2, T], at); at += 2 * T * 4
        pin = view("pin", [P, 2, TPAD], at); at += 2 * TPAD * 4
        sw = view("sw", [P, 1280], at); at += 1280 * 4
        rows = view("rows", [NH, 2 * TP + 3 * NS], at); at += (2 * TP + 3 * NS) * 4
        C_out = view("C_out", [P, NH, P], at); at += NH * P * 4
        wp_m = sb("wp_m", [P, 2, P])
        sw2 = view("sw2", [P, 1280], BT)
        h_tok = view("h_tok", [P, NH, NC, P + 1], BT + 5120)
        C_s = view("C_s", [P, NS, NH, P], 0, base=y_at)
        mem_h = view("mem_h", [P, KD, M], 0, F32R)
        mem_l = view("mem_l", [P, KD, M], 8192, F32R)
        mem = view("mem", [P, KD, M], 16384)
        mk = view("mk", [P, KD, M], 24576)
        mv = view("mv", [P, 2, D], 16384)
        qm = view("qm", [P, KD, T], 32768)
        k_ring = view("k_ring", [P, 2, KD, M], 49408)
        v_ring = view("v_ring", [P, 4, 2, D], 49408)
        prob = view("prob", [P, NC, M], 82176)
        probT = view("probT", [P, 2, TP], 86272)
        mvT = view("mvT", [P, KD, M], 82176)
        prob_s = view("prob_s", [NS, NH, M], 8192, base=y_at)
        q_one = view("q_one", [P, KD, NS, NS], 12288, base=y_at)
        p_one = view("p_one", [P, KD, NS, NS], 14336, base=y_at)
        o_rows = view("o_rows", [NS, D], 8192, base=y_at)

        ps = [ctx.enter_context(nc.psum_tensor(f"ps{n}", [P, 2, 512], F32)) for n in range(4)]

        s_x = signal("s_x")
        raw_landed = [signal(f"raw_landed{s}") for s in range(2)]
        hi_ready = signal("hi_ready", UNITS_LAYER)
        lo_ready = signal("lo_ready", UNITS_LAYER, 4)
        unit_done = signal("unit_done", UNITS_LAYER, 2)
        pair_evicted = [signal(f"pair_evicted{s}", EVICTED_LAYER, 1) for s in range(2)]
        silu_ready = signal("silu_ready", 2 * KF)
        hidden_hi = signal("hidden_hi", 2 * KF)
        hidden_lo = signal("hidden_lo", 2 * KF, 2)
        y_square = signal("y_square", 4 * KD)
        y_summed = signal("y_summed", 4 * (KD + 1), 1)
        msq_ready = signal("msq_ready", 4)
        root_ready = signal("root_ready", 8)
        x_even = signal("x_even", 4 * KD // 2, KD // 2)
        x_odd = signal("x_odd", 4 * KD // 2, KD // 2)
        y_scaled = signal("y_scaled", 3 * KD // 2)
        x_square = signal("x_square", 4 * KD)
        x_summed = signal("x_summed", 4 * KD)
        xn_ready = signal("xn_ready", 4 * KD)
        xh_ready = signal("xh_ready", 4 * KD)
        xl_even = signal("xl_even", 4 * KD // 2)
        xl_odd = signal("xl_odd", 4 * KD // 2)
        mix_loaded = signal("mix_loaded")
        C_loaded = signal("C_loaded")
        softplus_ready = signal("softplus_ready")
        mt_ready = signal("mt_ready")
        args_ready = signal("args_ready", 2)
        exps_ready = signal("exps_ready", 3)
        cols_done = signal("cols_done")
        cols_ready = signal("cols_ready", 2)
        tok_done = signal("tok_done", 4)
        ktok_ready = signal("ktok_ready", 2)
        vtok_ready = signal("vtok_ready", 2)
        head_scores = signal("head_scores", NH)
        d_ready = signal("d_ready", NH * NC)
        w_ready = signal("w_ready", NH * NC)
        sw_ready = signal("sw_ready", NH * NC)
        head_sums = signal("head_sums", NH)
        head_read = signal("head_read", NH)
        vones_ready = signal("vones_ready")
        h_mean = signal("h_mean")
        h_rooted = signal("h_rooted")
        htok_ready = signal("htok_ready")
        hT_done = signal("hT_done")
        hT_read = signal("hT_read")
        gb_done = signal("gb_done")
        gb_ready = signal("gb_ready", 2)
        kw_ready = signal("kw_ready")
        Cw_ready = signal("Cw_ready")
        C_done = signal("C_done")
        C_ready = signal("C_ready")
        qn_ready = signal("qn_ready")
        vrow_done = signal("vrow_done")
        vrow_ready = signal("vrow_ready")
        vb_done = signal("vb_done", NS)
        vkw_ready = signal("vkw_ready", NS)
        Cs_ready = signal("Cs_ready", NS)
        num_done = signal("num_done")
        dens_abs = signal("dens_abs")
        hs_ready = signal("hs_ready")
        h_square = signal("h_square")
        h_summed = signal("h_summed")
        h_root = signal("h_root")
        h_ready = signal("h_ready")
        win_zero = signal("win_zero")
        win_ready = signal("win_ready", 4)
        ws_ready = signal("ws_ready")
        diff_ready = signal("diff_ready")
        pooled = signal("pooled")
        pool_ready = signal("pool_ready", 2)
        mean_done = signal("mean_done")
        centered = signal("centered")
        c_square = signal("c_square", 2)
        var_done = signal("var_done")
        var_root = signal("var_root")
        vn_ready = signal("vn_ready")
        vnT_done = signal("vnT_done")
        vnT_ready = signal("vnT_ready")
        mixed_done = signal("mixed_done")
        gmlp_ready = signal("gmlp_ready")
        cat_hi = signal("cat_hi", 3)
        cat_lo = signal("cat_lo", 3)
        gate_ready = signal("gate_ready", 3 * KD)
        branch_done = signal("branch_done", 2 * KD)
        branch_read = signal("branch_read", 5 * KD, 5)
        mrg_hi = signal("mrg_hi", KD)
        mrg_lo = signal("mrg_lo", KD)
        out_mix = signal("out_mix")
        mem_first = signal("mem_first")
        mem_square = signal("mem_square")
        mem_summed = signal("mem_summed")
        mem_root = signal("mem_root")
        mem_inverse = signal("mem_inverse")
        mem_loaded = signal("mem_loaded")
        mem_scaled = signal("mem_scaled")
        mem_hi = signal("mem_hi", 2)
        mem_lo = signal("mem_lo", 2)
        sc_done = signal("sc_done", NH)
        max_ready = signal("max_ready", NH)
        p_ready = signal("p_ready", NH)
        pn_ready = signal("pn_ready", NH)
        pT_done = signal("pT_done", NH)
        pT_ready = signal("pT_ready", NH)
        o_done = signal("o_done", NH)
        oh_ready = signal("oh_ready", NH + 1)
        ol_ready = signal("ol_ready", NH + 1)
        k_landed = [signal(f"k_landed{s}", 4 * 16) for s in range(2)]
        v_landed = [signal(f"v_landed{s}", 2 * 16) for s in range(4)]
        k_used = signal("k_used", NS)
        v_used = signal("v_used", NS)
        mvT_done = signal("mvT_done")
        mv_ready = signal("mv_ready")
        q_one_ready = signal("q_one_ready")
        orow_ready = signal("orow_ready")
        oT_done = signal("oT_done")
        smax_ready = signal("smax_ready")
        sexp_ready = signal("sexp_ready")
        sp_ready = signal("sp_ready")
        spT_done = signal("spT_done")
        spT_ready = signal("spT_ready")
        out_mem = signal("out_mem")
        vec_ready = signal("vec_ready")
        scalar_step = signal("scalar_step", SCALAR_STEPS)
        vector_step = signal("vector_step", VECTOR_STEPS)
        out_y = signal("out_y")
        const_scaled = signal("const_scaled")
        zeros_ready = signal("zeros_ready")

        HALVES = [slice(0, HT), slice(HT, T)]

        def two(a):
            return a.rearrange("p (h t) -> p h t", h=2)

        def x_updated(l, sublayer, m):
            return (x_even, x_odd)[m % 2].at(l, sublayer * KD // 2 + m // 2 + 1)

        def xl_ready(l, norm, m):
            return (xl_even, xl_odd)[m % 2].at(l, norm * KD // 2 + m // 2 + 1)

        def post_tile(n):
            return 2 if n == 1 else 0

        def pre_tile(n):
            return 3 if n == PRE_ATT else 1

        sws = (sw, sw2)

        def score(h, j):
            bank, at = ((0, 0), (1, 0), (2, 0), (1, TP - P))[j]
            bank += 3 * (h % 2)
            return ps[bank // 2][:, bank % 2, at:at + TP - j * P]

        def done(phase, l, n):
            return unit_done.at(l, 4 * TURNS[phase] + n)

        def evicted(phase, s, l, n):
            return pair_evicted[s].at(l, EVICTED[phase] + n)

        block = ctx.enter_context(nc.Block())

        @block.sync
        def _(sp):
            sp.dma_start(ones[:], consts[:, 0:P]).then_inc(mem_first.sem, 16)
            sp.dma_start(mem[:], memT).then_inc(mem_first.sem, 16)
            sp.dma_start(x[:], xT).then_inc(s_x.sem, 16)
            sp.dma_start(vec_all[:], vecs).then_inc(s_x.sem, 16)
            for n, dst in enumerate((ident, neg_mask, causal)):
                sp.dma_start(dst[:], consts[:, (n + 1) * P:(n + 2) * P]).then_inc(s_x.sem, 16)
            at = 4 * P + 2 * PAD
            sp.dma_start(eye8[:], consts[:, at:at + NS * NS].rearrange("p (a b) -> p a b", a=NS))\
                .then_inc(s_x.sem, 16)
            sp.dma_start(early[:], consts[:, 4 * P:4 * P + 2 * PAD].rearrange("p (a b) -> p a b", a=2))\
                .then_inc(s_x.sem, 16)

            def pair(l, turn, s, src, n, behind=None):
                if behind:
                    sp.wait_ge(*behind)
                sp.wait_ge(*lo_ready.at(l, 4 * turn + 2 * s - 2))
                sp.dma_start(w_raw[:, s, 0:n * P], src).then_inc(raw_landed[s].sem, 16)

            def full(l, phase, i, turn0=0, behind=None, pairs=(0, 1)):
                for s in pairs:
                    src = sp.snap(l * FULL_PAIRS + (i * 2 + (FULL_AT[phase] + 2 * turn0 + s)))
                    pair(l, i + (TURNS[phase] + turn0), s,
                         w_full[bass.ds(src, 1), :, :].rearrange("a p n -> (a p) n"), 16,
                         behind)

            def down(l, phase, i, ffn):
                for s in range(2):
                    src = sp.snap(l * 32 + (i * 2 + (16 * ffn + s)))
                    pair(l, i + TURNS[phase], s, w_down[bass.ds(src, 1), :, :].rearrange("a p n -> (a p) n"), 11)

            def of(tensor, l):
                return tensor[bass.ds(l, 1)]

            def load_k(l, b):
                row = sp.snap(l * NS + b)
                if b == 0:
                    sp.wait_ge(*done("out", l, KD))
                if b >= 2:
                    sp.wait_ge(*k_used.at(l, b - 1))
                sp.dma_start(k_ring[:, b % 2, :, :], kT[bass.ds(row, 1)].rearrange("a p (k m) -> (a p) k m", k=KD))\
                    .then_inc(k_landed[b % 2].sem, 16)

            def load_v(l, b):
                row, slot = sp.snap(l * NS + b), (b + 2) % 4
                if b >= 4:
                    sp.wait_ge(*v_used.at(l, b - 3))
                elif b >= 2:
                    sp.wait_ge(*k_used.at(l, NS - 3 + b))
                sp.dma_start(v_ring[:, slot, :, :], vC[bass.ds(row, 1)].rearrange("a p (k m) -> (a p) k m", k=2))\
                    .then_inc(v_landed[slot].sem, 16)

            with sp.Fori(0, L) as l:
                with sp.Fori(0, 11) as i:
                    full(l, "up_a", i)
                with sp.Fori(0, 8) as i:
                    down(l, "down_a", i, 0)
                full(l, "in", 0)
                sp.wait_ge(*done("in", l, 0))
                for dst, src in ((ws_m, wsT), (bs_m, bsT), (wp_m, wpool), (pool_state, poolT), (n_state, nT),
                                 (m_state, mT)):
                    s = of(src, l)
                    sp.dma_start(dst[:], s.rearrange("l p (a b c) -> (l p) a b c", a=dst.shape[1], b=dst.shape[2])
                                 if len(dst.shape) == 4 else
                                 s.rearrange("l p (a b) -> (l p) a b", a=dst.shape[1])
                                 if len(dst.shape) == 3 else s.rearrange("l p a -> (l p) a"))\
                        .then_inc(mix_loaded.sem, 16)
                sp.wait_ge(*x_updated(l, 0, KD - 2))
                sp.dma_start(C_s[:], of(CT, l).rearrange("l p (a b c) -> (l p) a b c", a=NS, b=NH))\
                    .then_inc(C_loaded.sem, 16)
                with sp.Fori(1, 6) as i:
                    full(l, "in", i)
                full(l, "branch", 0)
                full(l, "branch", 0, 1, pairs=(0,))
                sp.wait_ge(*C_ready.at(l, 1))
                sp.dma_start(of(o_C, l).rearrange("l p n -> (l p) n"), C_out[:].rearrange("p a b -> p (a b)"))\
                    .then_inc(out_mix.sem, 16)
                sp.dma_start(of(o_n, l).rearrange("l p n -> (l p) n"), n_out[:]).then_inc(out_mix.sem, 16)
                sp.wait_ge(*Cs_ready.at(l, NS))
                sp.dma_start(of(o_CT, l).rearrange("l p n -> (l p) n"), C_s[:].rearrange("p a b c -> p (a b c)"))\
                    .then_inc(out_mix.sem, 16)
                sp.dma_start(of(o_nT, l).rearrange("l p n -> (l p) n"), n_state[:].rearrange("p a b -> p (a b)"))\
                    .then_inc(out_mix.sem, 16)
                sp.dma_start(of(o_m, l).rearrange("l p n -> (l p) n"), m_last[:]).then_inc(out_mix.sem, 16)
                sp.dma_start(of(o_mT, l).rearrange("l p n -> (l p) n"), m_new[:]).then_inc(out_mix.sem, 16)
                sp.dma_start(of(o_pool_p, l).rearrange("l p (a b) -> (l p) a b", a=2), pool_last[:])\
                    .then_inc(out_mix.sem, 16)
                sp.dma_start(of(o_pool_s, l).rearrange("l p n -> (l p) n"), pool_new[:].rearrange("p a b c -> p (a b c)"))\
                    .then_inc(out_mix.sem, 16)
                sp.dma_start(of(o_gv, l).rearrange("l p (a b) -> (l p) a b", a=2), gv_out[:])\
                    .then_inc(out_mix.sem, 16)
                full(l, "branch", 0, 1, pairs=(1,))
                with sp.Fori(2, 8) as i:
                    full(l, "branch", i)
                full(l, "out", 0)
                sp.wait_ge(*done("branch", l, 4 * KD))
                sp.dma_start(mem[:], memT).then_inc(mem_loaded.sem, 16)
                full(l, "out", 0, 1)
                full(l, "mk", 0)
                full(l, "mk", 0, 1)
                for b in range(2):
                    load_k(l, b)
                    load_v(l, b)
                with sp.Fori(0, 2) as i:
                    full(l, "mv", i)
                with sp.Fori(0, 2) as i:
                    full(l, "mq", i)
                full(l, "mo", 0)
                sp.wait_ge(*mv_ready.at(l, 1))
                sp.dma_start(of(o_mk, l).rearrange("l p n -> (l p) n"), mk[:].rearrange("p a b -> p (a b)"))\
                    .then_inc(out_mem.sem, 16)
                sp.dma_start(of(o_mv, l).rearrange("l p n -> (l p) n"), mv[:].rearrange("p a b -> p (a b)"))\
                    .then_inc(out_mem.sem, 16)
                for b in range(2, NS):
                    load_k(l, b)
                for b in range(2, NS):
                    load_v(l, b)
                full(l, "mo", 0, 1)
                with sp.Fori(0, 11) as i:
                    full(l, "up_b", i)
                with sp.Fori(0, 8) as i:
                    down(l, "down_b", i, 1)
            sp.wait_ge(*x_updated(L - 1, 3, KD - 2))
            sp.wait_ge(*x_updated(L - 1, 3, KD - 1))
            sp.dma_start(o_y, x[:]).then_inc(out_y.sem, 16)
            sp.wait_ge(out_y.sem, 16)
            sp.wait_ge(out_mix.sem, L * 144)
            sp.wait_ge(out_mem.sem, L * 32)

        @block.gpsimd
        def _(pool):
            pool.sem_inc(lo_ready.sem, lo_ready.credit)

            def lo(l, turn, s, tiles):
                at = 0
                for u, n in enumerate(tiles[s]):
                    pool.wait_ge(*hi_ready.at(l, turn * 4 + (2 * s + u + 1)))
                    pool.tensor_tensor(w_lo[:, u, 0:n * P], w_raw[:, s, at:at + n * P],
                                       w_hi[:, u, 0:n * P].bitcast(F32), ALU.subtract).then_inc(lo_ready.sem, 1)
                    at += n * P

            def turns(l, first, n, tiles):
                if n == 1:
                    lo(l, first, 0, tiles)
                    lo(l, first, 1, tiles)
                    return
                with pool.Fori(0, n) as i:
                    for s in range(2):
                        lo(l, i + first, s, tiles)

            def post_odd(l, n):
                for m in range(1, KD, 2):
                    pool.wait_ge(*y_scaled.at(l, (0, None, 1, 2)[n] * KD // 2 + m // 2 + 1))
                    pool.tensor_tensor(x[:, m, :], x[:, m, :], tmp[1][:], ALU.add).then_inc(x_odd.sem, 1)

            def pre_odd(l, n):
                for m in range(1, KD, 2):
                    pool.wait_ge(*xh_ready.at(l, n * KD + m + 1))
                    pool.tensor_tensor(xl[:, m, :], tmp[1][:], xh[:, m, :].bitcast(F32), ALU.subtract)\
                        .then_inc(xl_odd.sem, 1)

            with pool.Fori(0, L) as l:
                lo(l, TURNS["up_a"], 0, FULL)
                pre_odd(l, PRE_A)
                lo(l, TURNS["up_a"], 1, FULL)
                turns(l, TURNS["up_a"] + 1, 10, FULL)
                turns(l, TURNS["down_a"], 8, DOWN)
                lo(l, TURNS["in"], 0, FULL)
                post_odd(l, 0)
                pre_odd(l, PRE_MIX)
                lo(l, TURNS["in"], 1, FULL)
                turns(l, TURNS["in"] + 1, 1, FULL)
                pool.wait_ge(*evicted("in", 1, l, 1))
                pool.wait_ge(*win_zero.at(l, 1))
                pool.tensor_tensor(winA[:, :, 2:528], pin[:, :, 2:528], pin[:, :, 1:527], ALU.add)\
                    .then_inc(win_ready.sem, 1)
                turns(l, TURNS["in"] + 2, 1, FULL)
                pool.wait_ge(*win_ready.at(l, 1))
                pool.tensor_tensor(winB[:, :, 4:528], winA[:, :, 4:528], winA[:, :, 2:526], ALU.add)\
                    .then_inc(win_ready.sem, 1)
                turns(l, TURNS["in"] + 3, 1, FULL)
                pool.wait_ge(*win_ready.at(l, 2))
                pool.tensor_tensor(winA[:, 1, 8:528], winB[:, 1, 8:528], winB[:, 1, 4:524], ALU.add)\
                    .then_inc(win_ready.sem, 1)
                pool.wait_ge(*win_ready.at(l, 3))
                pool.tensor_tensor(winB[:, 1, 16:528], winA[:, 1, 16:528], winA[:, 1, 8:520], ALU.add)\
                    .then_inc(win_ready.sem, 1)
                turns(l, TURNS["in"] + 4, 1, FULL)
                pool.wait_ge(mix_loaded.sem, l * 96 + 96)
                pool.tensor_tensor(ws_m[:], ws_m[:], causal[:].unsqueeze(1).to_broadcast([P, 4, P]), ALU.mult)\
                    .then_inc(ws_ready.sem, 1)
                turns(l, TURNS["in"] + 5, 1, FULL)
                lo(l, TURNS["branch"], 0, FULL)
                pool.wait_ge(*cols_ready.at(l, 2))
                pool.wait_ge(*ktok_ready.at(l, 2))
                pool.tensor_tensor(k_tok[:], k_tok[:],
                                   cols[:, 1, :, :].rearrange("p j h -> p h j").unsqueeze(3)
                                   .to_broadcast([P, NH, NC, P]), ALU.mult).then_inc(kw_ready.sem, 1)
                pool.wait_ge(C_loaded.sem, l * 16 + 16)
                pool.tensor_tensor(C_s[:], C_s[:], s_rows[:, :, 0, :].rearrange("p h b -> p b h").unsqueeze(3)
                                   .to_broadcast([P, NS, NH, P]), ALU.mult).then_inc(Cw_ready.sem, 1)
                lo(l, TURNS["branch"], 1, FULL)
                turns(l, TURNS["branch"] + 1, TURNS["up_b"] - TURNS["branch"] - 1, FULL)
                lo(l, TURNS["up_b"], 0, FULL)
                post_odd(l, 2)
                pre_odd(l, PRE_B)
                lo(l, TURNS["up_b"], 1, FULL)
                turns(l, TURNS["up_b"] + 1, 10, FULL)
                turns(l, TURNS["down_b"], 8, DOWN)
                post_odd(l, 3)

        @block.tensor
        def _(pe):
            pe.wait_ge(zeros_ready.sem, 1)
            pe.wait_ge(mem_first.sem, 32)
            pe.wait_ge(mem_square.sem, 1)
            for m in range(KD):
                r = pe.matmul(ps[2][:, 0, 0:M], ones[:], mem[:, m, :], start=m == 0, stop=m == KD - 1)
            r.then_inc(mem_summed.sem, 1)
            pe.wait_ge(s_x.sem, 7 * 16)
            pe.sem_inc(unit_done.sem, unit_done.credit)

            def unit(l, turn, s, u, tiles, out, rhs, start=True, stop=True, ready=None):
                pe.wait_ge(*lo_ready.at(l, turn * 4 + (2 * s + u + 1)))
                last = None
                for n in range(tiles):
                    if ready:
                        pe.wait_ge(*ready(n))
                    w = slice(n * P, (n + 1) * P)
                    ah, al = rhs(n)
                    for c, (wt, a) in enumerate(((w_hi, al), (w_hi, ah), (w_lo, ah))):
                        for h in range(2):
                            last = pe.matmul(out[:, h, 0:HT], wt[:, u, w], a[:, HALVES[h]],
                                             start=start and n == 0 and c == 0,
                                             stop=stop and n == tiles - 1 and c == 2)
                return last

            def of_x(n):
                return xh[:, n, :], xl[:, n, :]

            def linear(l, phase, turns, rhs, ready, behind=None):
                with pe.Fori(0, turns) as i:
                    if behind:
                        pe.wait_ge(*behind)
                    for s in range(2):
                        pe.wait_ge(*evicted(phase, s, l, i))
                        for u in range(2):
                            unit(l, i + TURNS[phase], s, u, KD, ps[2 * s + u], rhs,
                                 ready=ready if s == u == 0 else None).then_inc(unit_done.sem, 1)

            def ffn(l, up, down, ffn_index):
                linear(l, up, 11, of_x, lambda n: xl_ready(l, (PRE_A, PRE_B)[ffn_index], n))
                with pe.Fori(0, 4) as i:
                    for mm in range(2):
                        pe.wait_ge(*evicted(down, mm, l, i))
                        at = 0
                        for s in range(2):
                            for u in range(2):
                                first = at
                                unit(l, i * 2 + (TURNS[down] + mm), s, u, DOWN[s][u], ps[2 * mm],
                                     lambda n: (hid_h[:, first + n, :], hid_l[:, first + n, :]),
                                     start=at == 0, stop=at + DOWN[s][u] == KF,
                                     ready=None if mm else lambda n: hidden_lo.at(l, ffn_index * KF + first + n + 1))\
                                    .then_inc(unit_done.sem, 1)
                                at += DOWN[s][u]

            def sum_partitions(out, a, first, last):
                for h in range(2):
                    r = pe.matmul(out[:, h, 0:HT], ones[:], a[:, HALVES[h]], start=first, stop=last)
                return r

            def post(l, n):
                pe.wait_ge(*y_summed.at(l, (n + 1) * (KD + 1)))
                sum_partitions(ps[post_tile(n)], ssq, True, True).then_inc(msq_ready.sem, 1)

            def pre(l, n):
                for m in range(KD):
                    pe.wait_ge(*x_square.at(l, n * KD + m + 1))
                    sum_partitions(ps[pre_tile(n)], tmp[2 + m % 2], m == 0, m == KD - 1).then_inc(x_summed.sem, 1)

            def mixer(l):
                pe.wait_ge(*evicted("in", 0, l, 6))
                pe.wait_ge(*evicted("in", 1, l, 6))
                for j in range(2):
                    r = sum_partitions(ps[2], gv[:, j, :], j == 0, j == 1)
                r.then_inc(mean_done.sem, 1)
                for t in range(2):
                    for b in range(2):
                        for c in range(NC):
                            r = pe.transpose(ps[t][:, b, c * P:(c + 1) * P],
                                             k[:, (2 * t + b), c * P:(c + 1) * P], ident[:])
                    r.then_inc(tok_done.sem, 1)
                pe.wait_ge(*exps_ready.at(l, 3))
                for h in range(NH):
                    pe.matmul(ps[3][:, 1, 24 * h:24 * h + 24], ident[0:NH, h:h + 1].to_broadcast([NH, P]),
                              rows[:, 2 * TP:], start=True, stop=True)
                for n, src in enumerate((rms, tmp[1], rows[:, TP:])):
                    for c in range(NC):
                        r = pe.transpose(ps[3][:, 0, 16 * n + 4 * c:16 * n + 4 * c + 4],
                                         src[0:NH, c * P:(c + 1) * P], ident[0:NH, 0:NH])
                r.then_inc(cols_done.sem, 1)
                pe.wait_ge(*c_square.at(l, 2))
                for j in range(2):
                    r = sum_partitions(ps[2], tmp[2 + j], j == 0, j == 1)
                r.then_inc(var_done.sem, 1)
                for t in range(2):
                    pe.wait_ge(*ktok_ready.at(l, t + 1))
                    for b in range(2):
                        for c in range(NC):
                            r = pe.transpose(ps[t][:, b, c * P:(c + 1) * P],
                                             v[:, (2 * t + b), c * P:(c + 1) * P], ident[:])
                    r.then_inc(tok_done.sem, 1)
                pe.wait_ge(*vtok_ready.at(l, 2))
                for h in range(NH):
                    r = pe.matmul(ps[h // 2][:, h % 2, :], ident[0:NH, h:h + 1].to_broadcast([NH, P]), rows[:, 0:TP],
                                  start=True, stop=True)
                r.then_inc(gb_done.sem, 1)
                pe.wait_ge(*vn_ready.at(l, 1))
                for c in range(NC):
                    for j in range(2):
                        r = pe.transpose(ps[2][:, c // 2, (c % 2) * 256 + j * P:(c % 2) * 256 + (j + 1) * P],
                                         gv[:, j, c * P:(c + 1) * P], ident[:])
                r.then_inc(vnT_done.sem, 1)
                pe.wait_ge(*cols_ready.at(l, 2))
                pe.wait_ge(*vnT_ready.at(l, 1))
                pe.wait_ge(*ws_ready.at(l, 1))
                for g in range(4):
                    j, half = g // 2, slice(64 * (g % 2), 64 * (g % 2) + 64)
                    for c in range(NC):
                        r = pe.matmul(ps[3][half, j, c * P:(c + 1) * P], vn_tok[:, c, g * 64:(g + 1) * 64],
                                      ws_m[:, g, :], start=True, stop=True)
                r.then_inc(mixed_done.sem, 1)

                pe.wait_ge(*gb_ready.at(l, 2))
                pe.wait_ge(*diff_ready.at(l, 1))
                for j in range(2):
                    for h in range(2):
                        r = pe.matmul(ps[j][:, h, 0:HT], wp_m[:, j, :],
                                      winA[:, j, PAD + h * HT:PAD + (h + 1) * HT], start=True, stop=True)
                r.then_inc(pooled.sem, 1)
                pe.wait_ge(*pool_ready.at(l, 2))
                pe.wait_ge(*gmlp_ready.at(l, 1))
                def head_products(h):
                    for j in range(NC):
                        r = pe.matmul(score(h, j), k[:, h, j * P:(j + 1) * P], q[:, h, j * P:TP],
                                      start=True, stop=True)
                    r.then_inc(head_scores.sem, 1)

                head_products(0)
                pe.wait_ge(*vones_ready.at(l, 1))
                head_products(1)
                for h in range(NH):
                    if h:
                        pe.wait_ge(*head_read.at(l, h))
                    for i in range(NC):
                        pe.wait_ge(*sw_ready.at(l, h * NC + i + 1))
                        for j in range(i + 1):
                            at = j * TP - P * (j * (j - 1) // 2) + (i - j) * P
                            r = pe.matmul(ps[3][:, i // 2, (i % 2) * (P + 1):(i % 2 + 1) * (P + 1)],
                                          sws[h % 2][:, at:at + P], v_tok[:, h, j, :], start=j == 0, stop=j == i)
                    r.then_inc(head_sums.sem, 1)
                    if h + 2 < NH:
                        head_products(h + 2)
                pe.wait_ge(*kw_ready.at(l, 1))
                for h in range(NH):
                    for j in range(NC):
                        pe.matmul(ps[0][:, 0, h * P:(h + 1) * P], v_tok[:, h, j, 0:P], k_tok[:, h, j, :],
                                  start=j == 0, stop=j == NC - 1)
                    for j in range(NC):
                        r = pe.matmul(ps[0][:, 1, h:h + 1], k_tok[:, h, j, :], ones[:, 0:1],
                                      start=j == 0, stop=j == NC - 1)
                r.then_inc(C_done.sem, 1)
                for h in range(NH):
                    r = pe.transpose(ps[1][0:NS, 0, h * P:(h + 1) * P], v[:, h, TP:T], ident[:])
                r.then_inc(vrow_done.sem, 1)
                pe.wait_ge(*qn_ready.at(l, 1))
                pe.wait_ge(*head_read.at(l, NH))
                pe.matmul(ps[3][:, 1, 0:NH * NS], ones[:], qn_s[:].rearrange("p a b -> p (a b)"),
                          start=True, stop=True)
                pe.wait_ge(*C_ready.at(l, 1))
                pe.wait_ge(*vrow_ready.at(l, 1))
                pe.wait_ge(*htok_ready.at(l, 1))
                for h in range(NH):
                    for c in range(NC):
                        r = pe.transpose(ps[h // 2][:, h % 2, c * P:(c + 1) * P], h_tok[:, h, c, 0:P], ident[:])
                r.then_inc(hT_done.sem, 1)
                for b in range(NS + 2):
                    if b < NS:
                        if b >= 2:
                            pe.wait_ge(*(vkw_ready.at(l, b - 3) if b >= 4 else hT_read.at(l, 1)))
                        pe.matmul(ps[2 - b // 2 % 2][:, b % 2, :], ident[0:NS, b:b + 1].to_broadcast([NS, P]),
                                  tmp[2][0:NS, 0:TP], start=True, stop=True).then_inc(vb_done.sem, 1)
                    if b >= 2:
                        pe.wait_ge(*Cs_ready.at(l, b - 1))
                        for h in range(NH):
                            at = h * NS + b - 2
                            r = pe.matmul(ps[3][:, 0, at:at + 1], C_s[:, b - 2, h, :],
                                          q[:, h, TP + b - 2:TP + b - 1], start=True, stop=True)
                r.then_inc(num_done.sem, 1)
                pe.wait_ge(*h_square.at(l, 1))
                pe.matmul(ps[3][:, 1, 0:NH * NS], ones[:], tmp[3][:, 0:NH * NS], start=True, stop=True)\
                    .then_inc(h_summed.sem, 1)

            def of_cat(first):
                return lambda n: (cat_h[:, first + n, :], cat_l[:, first + n, :])

            def branches(l):
                with pe.Fori(0, KD) as m:
                    turn = m + TURNS["branch"]
                    pe.wait_ge(*hT_read.at(l, 1))
                    pe.wait_ge(*branch_read.at(l, m * 5 - 4))
                    unit(l, turn, 0, 0, KD, ps[0], of_x).then_inc(unit_done.sem, 1)
                    pe.wait_ge(*branch_read.at(l, m * 5 - 3))
                    unit(l, turn, 0, 1, KD, ps[1], of_x).then_inc(unit_done.sem, 1)
                    pe.wait_ge(*branch_read.at(l, m * 5 - 2))
                    unit(l, turn, 1, 0, KD, ps[2], of_x).then_inc(unit_done.sem, 1)
                    pe.wait_ge(*lo_ready.at(l, turn * 4 + 4))
                    pe.wait_ge(*cat_lo.at(l, 3))

                    def branch(out, first, n):
                        last = None
                        for c in range(n):
                            w = slice((first + c) * P, (first + c + 1) * P)
                            for t, (wt, a) in enumerate(((w_hi, cat_l), (w_hi, cat_h), (w_lo, cat_h))):
                                for h in range(2):
                                    last = pe.matmul(out[:, h, 0:HT], wt[:, 1, w], a[:, first + c, HALVES[h]],
                                                     start=c == 0 and t == 0, stop=c == n - 1 and t == 2)
                        return last

                    pe.wait_ge(*gate_ready.at(l, m * 3 + 2))
                    branch(ps[0], 2, 4).then_inc(branch_done.sem, 1)
                    branch(ps[1], 6, 2).then_inc(branch_done.sem, 1)
                    branch(ps[3], 0, 2).then_inc(unit_done.sem, 1)

            def memory(l):
                def unit_kv(phase, i, s, u):
                    if u == 0:
                        pe.wait_ge(*evicted(phase, s, l, i))
                    pe.wait_ge(*lo_ready.at(l, i * 4 + (4 * TURNS[phase] + 2 * s + u + 1)))
                    for n in range(KD):
                        w = slice(n * P, (n + 1) * P)
                        for c, (wt, a) in enumerate(((w_hi, mem_l), (w_hi, mem_h), (w_lo, mem_h))):
                            r = pe.matmul(ps[s][:, u, 0:M], wt[:, u, w], a[:, n, :],
                                          start=n == 0 and c == 0, stop=n == KD - 1 and c == 2)
                    r.then_inc(unit_done.sem, 1)

                n = PRE_ATT

                def sums(*tiles):
                    for m in tiles:
                        pe.wait_ge(*x_square.at(l, PRE_ATT * KD + m + 1))
                        sum_partitions(ps[pre_tile(n)], tmp[2 + m % 2], m == 0, m == KD - 1).then_inc(x_summed.sem, 1)

                pe.wait_ge(*mem_lo.at(l, 2))
                unit_kv("mk", 0, 0, 0)
                post(l, 1)
                unit_kv("mk", 0, 0, 1)
                unit_kv("mk", 0, 1, 0)
                unit_kv("mk", 0, 1, 1)
                sums(0, 1)
                unit_kv("mk", 1, 0, 0)
                sums(2, 3)
                unit_kv("mk", 1, 0, 1)
                sums(4, 5, 6, 7)
                unit_kv("mk", 1, 1, 0)
                unit_kv("mk", 1, 1, 1)
                with pe.Fori(0, 2) as i:
                    for s in range(2):
                        for u in range(2):
                            unit_kv("mv", i, s, u)

            def attention(l):
                for s in range(2):
                    pe.wait_ge(*evicted("mq", s, l, 2))

                def scores(h):
                    for t in range(NC):
                        for d in range(2):
                            r = pe.matmul(ps[h % 2][:, t // 2, (t % 2) * M:(t % 2 + 1) * M],
                                          qm[:, 2 * h + d, t * P:(t + 1) * P], mk[:, 2 * h + d, :],
                                          start=d == 0, stop=d == 1)
                    r.then_inc(sc_done.sem, 1)

                def sample_zero():
                    for j in range(2):
                        pe.matmul(ps[3][0:NS, j, :], zeros8[:], x[:, j, 0:TP], start=True, stop=False)

                def sample_scores(b):
                    pe.wait_ge(k_landed[b % 2].sem, l * 64 + 16 * (b // 2 + 1))
                    for f in range(KD):
                        h = f // 2
                        r = pe.matmul(ps[3][0:NS, h // 2, (h % 2) * M:(h % 2 + 1) * M], q_one[:, f, b, :],
                                      k_ring[:, b % 2, f, :], start=False, stop=b == NS - 1 and f % 4 == 3)
                    r.then_inc(k_used.sem, 1)

                def sample_values(b):
                    slot = (b + 2) % 4
                    pe.wait_ge(v_landed[slot].sem, l * 32 + 16 * (b // 4 + 1))
                    for h in range(NH):
                        for mt in range(2):
                            r = pe.matmul(ps[3][0:NS, h // 2, (h % 2) * M:(h % 2 + 1) * M], p_one[:, 2 * h + mt, b, :],
                                          v_ring[:, slot, mt, h * M:(h + 1) * M], start=False,
                                          stop=b == NS - 1 and h % 2 == 1 and mt == 1)
                    r.then_inc(v_used.sem, 1)

                scores(0)
                for mt in range(2):
                    for f in range(KD):
                        r = pe.transpose(ps[2 + mt][:, f // 4, (f % 4) * P:(f % 4 + 1) * P],
                                         mvT[:, f, mt * P:(mt + 1) * P], ident[:])
                r.then_inc(mvT_done.sem, 1)
                scores(1)
                pe.wait_ge(*mv_ready.at(l, 1))
                pe.wait_ge(*q_one_ready.at(l, 1))
                sample_zero()
                sample_scores(0)
                for h in range(NH):
                    sc = ps[h % 2]
                    pe.wait_ge(*pn_ready.at(l, h + 1))
                    for t in range(NC):
                        for mt in range(2):
                            r = pe.transpose(ps[2][:, mt, t * P:(t + 1) * P], prob[:, t, mt * P:(mt + 1) * P], ident[:])
                    r.then_inc(pT_done.sem, 1)
                    if h < 3:
                        sample_scores(2 * h + 1)
                    pe.wait_ge(*pT_ready.at(l, h + 1))
                    for d in range(2):
                        for mt in range(2):
                            r = pe.matmul(sc[:, d, :], mv[:, mt, (2 * h + d) * P:(2 * h + d + 1) * P],
                                          probT[:, mt, :], start=mt == 0, stop=mt == 1)
                    r.then_inc(o_done.sem, 1)
                    if h < 3:
                        sample_scores(2 * h + 2)
                    if h == 2:
                        sample_scores(NS - 1)
                    if h < 2:
                        pe.wait_ge(*ol_ready.at(l, h + 1))
                        scores(h + 2)
                pe.wait_ge(*sp_ready.at(l, 1))
                for f in range(KD):
                    r = pe.matmul(ps[3][:, 0, f * NS:(f + 1) * NS], prob_s[:, f // 2, (f % 2) * P:(f % 2 + 1) * P],
                                  ident[0:NS, 0:NS], start=True, stop=True)
                r.then_inc(spT_done.sem, 1)
                pe.wait_ge(*spT_ready.at(l, 1))
                sample_zero()
                for b in range(NS):
                    sample_values(b)
                pe.wait_ge(*orow_ready.at(l, 1))
                for f in range(KD):
                    r = pe.matmul(ps[2][:, 0, f * NS:(f + 1) * NS], o_rows[:, f * P:(f + 1) * P],
                                  ident[0:NS, 0:NS], start=True, stop=True)
                r.then_inc(oT_done.sem, 1)

            with pe.Fori(0, L) as l:
                pre(l, 0)
                ffn(l, "up_a", "down_a", 0)
                post(l, 0)
                pre(l, 1)
                linear(l, "in", 6, of_x, lambda n: xl_ready(l, PRE_MIX, n))
                mixer(l)
                branches(l)
                linear(l, "out", 2, lambda n: (mrg_h[:, n, :], mrg_l[:, n, :]), lambda n: mrg_lo.at(l, n + 1),
                       branch_read.at(l, 5 * KD - 2))
                memory(l)
                linear(l, "mq", 2, of_x, lambda n: xl_ready(l, PRE_ATT, n), evicted("mq", 1, l, 0))
                attention(l)
                linear(l, "mo", 2, of_x, None, ol_ready.at(l, NH + 1))
                post(l, 2)
                pre(l, PRE_B)
                ffn(l, "up_b", "down_b", 1)
                post(l, 3)

        @block.scalar
        def _(act):
            own = Steps(act, scalar_step)

            def hi(l, turn, s, tiles):
                act.wait_ge(raw_landed[s].sem, (l * TURNS_LAYER + turn) * 16 + 16)
                at = 0
                for u, n in enumerate(tiles[s]):
                    act.wait_ge(*unit_done.at(l, turn * 4 + (2 * s + u - 1)))
                    act.activation(w_hi[:, u, 0:n * P], w_raw[:, s, at:at + n * P], ACT.Copy)\
                        .then_inc(hi_ready.sem, 1)
                    at += n * P

            def stream(l, phase, n, tiles, evict, after, ahead=False, between=None):
                def turn(i, last):
                    for s in range(2):
                        if s == 0:
                            if not (ahead and isinstance(i, int) and i == 0):
                                hi(l, i + TURNS[phase], 1, tiles)
                        elif not last:
                            hi(l, i + (TURNS[phase] + 1), 0, tiles)
                        elif after:
                            hi(l, TURNS[phase] + n, 0, after)
                        evict(i, s)

                if ahead:
                    turn(0, False)
                with act.Fori(1 if ahead else 0, n - 1) as i:
                    turn(i, False)
                if between:
                    between(l)
                turn(n - 1, True)

            def squares(l, group, phase):
                def evict(i, s):
                    for u in range(2):
                        m = i * 4 + (2 * s + u)
                        act.wait_ge(*done(phase, l, m + 1))
                        act.wait_ge(*y_summed.at(l, m + group * (KD + 1)))
                        act.activation(two(tmp[u][:]), ps[2 * s + u][:, :, 0:HT], ACT.Square)\
                            .then_inc(y_square.sem, 1)
                return evict

            def ffn(l, n, up, down, after):
                def evict(i, s):
                    f = i * 2 + s
                    act.wait_ge(*done(up, l, i * 4 + (2 * s + 1)))
                    act.wait_ge(*evicted(up, s, l, i))
                    act.activation(two(tmp[s][:]), ps[2 * s][:, :, 0:HT], ACT.Silu).then_inc(silu_ready.sem, 1)
                    act.wait_ge(*evicted(up, s, l, i + 1))
                    act.activation(hid_h[:, bass.ds(f, 1) if not isinstance(f, int) else slice(f, f + 1), :],
                                   tmp[2 + s][:].unsqueeze(1), ACT.Copy).then_inc(hidden_hi.sem, 1)

                stream(l, up, 11, FULL, evict, DOWN)

                def turn(i, mm, last):
                    t = i * 2 + (TURNS[down] + mm)
                    hi(l, t, 1, DOWN)
                    if not last:
                        hi(l, t + 1, 0, DOWN)
                    elif after:
                        hi(l, t + 1, 0, after)
                    m = i * 2 + mm
                    act.wait_ge(*done(down, l, m * 4 + 4))
                    act.wait_ge(*y_summed.at(l, m + 3 * n * (KD + 1)))
                    act.activation(two(tmp[mm][:]), ps[2 * mm][:, :, 0:HT], ACT.Square).then_inc(y_square.sem, 1)

                with act.Fori(0, 3) as i:
                    for mm in range(2):
                        turn(i, mm, False)
                turn(3, 0, False)
                turn(3, 1, True)

            def post(l, n):
                act.wait_ge(*msq_ready.at(l, n + 1))
                act.activation(two(rms[:]), ps[post_tile(n)][:, :, 0:HT], ACT.Sqrt, bias=EPS, scale=1.0 / D)\
                    .then_inc(root_ready.sem, 1)

            def pre_squares(l, n, sublayer, tiles):
                for m in tiles:
                    act.wait_ge(*x_updated(l, sublayer - 1, m))
                    if m >= 2:
                        act.wait_ge(*x_summed.at(l, n * KD + m - 1))
                    act.activation(tmp[2 + m % 2][:], x[:, m, :], ACT.Square).then_inc(x_square.sem, 1)

            def pre_root(l, n):
                act.wait_ge(*x_summed.at(l, (n + 1) * KD))
                act.activation(two(rms[:]), ps[pre_tile(n)][:, :, 0:HT], ACT.Sqrt, bias=EPS, scale=1.0 / D)\
                    .then_inc(root_ready.sem, 1)

            def pre_hi(l, n, tiles):
                for m in tiles:
                    act.wait_ge(*xn_ready.at(l, n * KD + m + 1))
                    act.activation(xh[:, m, :], tmp[m % 2][:], ACT.Copy).then_inc(xh_ready.sem, 1)

            def pre(l, n, sublayer):
                if sublayer == 0:
                    act.wait_ge(s_x.sem, 7 * 16)
                pre_squares(l, n, sublayer, range(KD))
                pre_root(l, n)
                pre_hi(l, n, range(KD))

            def evict_in(l):
                kinds = (("gates", 0), ("pool", 0), ("u", 0), ("gv", 0), ("o", 0), ("o", 2), ("q", 0), ("q", 2),
                         ("k", 0), ("k", 2), ("v", 0), ("v", 2))

                def evict(i, s):
                    kind, at = kinds[2 * i + s]
                    if kind == "gates":
                        return
                    for u in range(2):
                        act.wait_ge(*done("in", l, 4 * i + 2 * s + u + 1))
                        src = ps[2 * s + u][:, :, 0:HT]
                        if kind == "pool":
                            r = act.activation(two(pin[:, u, PAD:TPAD]), src, ACT.Copy)
                        elif kind in ("q", "v"):
                            r = act.activation(two({"q": q, "v": v}[kind][:, at + u, :]), src, ACT.Copy)
                        elif kind == "k":
                            r = act.activation(two(k[:, at + u, :]), src, ACT.Copy, scale=float(P) ** -0.5)
                        elif kind == "o":
                            r = act.activation(two(og[:, at + u, :]), src, ACT.Sigmoid)
                        else:
                            r = act.activation(two({"u": gu, "gv": gv}[kind][:, u, :]), src, ACT.Gelu_apprx_tanh)
                        if u:
                            r.then_inc(pair_evicted[s].sem, 1)
                return evict

            def softplus(l):
                act.wait_ge(*evicted("in", 0, l, 1))
                f, e = tmp[1][0:NH, :], tmp[2][0:NH, :]
                own.link(act.activation(e, f, ACT.Abs))
                own.link(act.activation(e, e, ACT.Exp, scale=-1.0))
                act.activation(e, e, ACT.Ln, bias=1.0).then_inc(softplus_ready.sem, 1)

            def gate_exps(l):
                act.wait_ge(*mt_ready.at(l, 1))
                act.activation(rows[:, TP:2 * TP], tmp[3][0:NH, 0:TP], ACT.Exp, scale=-1.0)\
                    .then_inc(exps_ready.sem, 1)
                act.wait_ge(*args_ready.at(l, 1))
                act.activation(rows[:, 2 * TP:], m_args[:].rearrange("p a b -> p (a b)"), ACT.Exp)\
                    .then_inc(exps_ready.sem, 1)
                act.wait_ge(*args_ready.at(l, 2))
                act.activation(tmp[1][0:NH, 0:TP], tmp[1][0:NH, 0:TP], ACT.Exp).then_inc(exps_ready.sem, 1)

            def mixer(l):
                act.wait_ge(*centered.at(l, 1))
                for j in range(2):
                    act.activation(tmp[2 + j][:], gv[:, j, :], ACT.Square).then_inc(c_square.sem, 1)
                for t in range(2):
                    act.wait_ge(*tok_done.at(l, t + 1))
                    act.activation(k_tok[:, 2 * t:2 * t + 2, :, :].rearrange("p a b c -> p a (b c)"), ps[t][:],
                                   ACT.Copy).then_inc(ktok_ready.sem, 1)
                act.wait_ge(*var_done.at(l, 1))
                act.activation(two(tmp[2][:]), ps[2][:, :, 0:HT], ACT.Sqrt, bias=LN_EPS, scale=1.0 / 256)\
                    .then_inc(var_root.sem, 1)
                act.wait_ge(*gb_done.at(l, 1))
                for t in range(2):
                    act.activation(v[:, 2 * t:2 * t + 2, 0:TP], ps[t][:], ACT.Copy).then_inc(gb_ready.sem, 1)
                act.wait_ge(*vnT_done.at(l, 1))
                act.activation(vn_tok[:].rearrange("p (b c) n -> p b (c n)", b=2), ps[2][:], ACT.Copy)\
                    .then_inc(vnT_ready.sem, 1)
                act.wait_ge(*pooled.at(l, 1))
                act.wait_ge(*gmlp_ready.at(l, 1))
                act.wait_ge(*vec_ready.at(l, 1))
                for j in range(2):
                    act.activation(two(gv[:, j, :]), ps[j][:, :, 0:HT], ACT.Copy,
                                   scale=vec[:, V_SPOOL + j:V_SPOOL + j + 1]).then_inc(pool_ready.sem, 1)
                def weights(h):
                    at = 0
                    for j in range(NC):
                        n = TP - j * P
                        act.wait_ge(*d_ready.at(l, h * NC + j + 1))
                        act.activation(sws[h % 2][:, at:at + n], sws[h % 2][:, at:at + n], ACT.Exp)\
                            .then_inc(w_ready.sem, 1)
                        at += n

                weights(0)
                for h in range(NH):
                    if h + 1 < NH:
                        weights(h + 1)
                    act.wait_ge(*head_sums.at(l, h + 1))
                    own.mark(act.activation(h_tok[:, h, :, :].rearrange("p (a b) n -> p a (b n)", a=2),
                                            ps[3][:, :, 0:2 * (P + 1)], ACT.Copy))
                    for c in range(NC):
                        at = (c % 2) * (P + 1)
                        r = act.activation(tmp[0][:, c * P:(c + 1) * P], ps[3][:, c // 2, at:at + P], ACT.Square,
                                           accum_out=h_sum[:, h, c:c + 1])
                        if c < NC - 1:
                            own.mark(r)
                    r.then_inc(head_read.sem, 1)
                    if h + 1 < NH:
                        own.settle()
                act.wait_ge(*h_mean.at(l, 1))
                act.activation(h_rms[:], h_rms[:], ACT.Sqrt, bias=EPS, scale=1.0 / P).then_inc(h_rooted.sem, 1)
                act.wait_ge(*C_done.at(l, 1))
                own.mark(act.activation(C_out[:].rearrange("p a b -> p (a b)"), ps[0][:, 0, :], ACT.Copy))
                act.activation(n_out[:], ps[0][:, 1, 0:NH], ACT.Copy).then_inc(C_ready.sem, 1)
                act.wait_ge(*vrow_done.at(l, 1))
                act.activation(tmp[2][0:NS, 0:TP], ps[1][0:NS, 0, :], ACT.Copy).then_inc(vrow_ready.sem, 1)
                for b in range(NS):
                    act.wait_ge(*vb_done.at(l, b + 1))
                    if b >= 2:
                        act.wait_ge(*Cs_ready.at(l, b - 1))
                    for h in range(NH):
                        r = act.activation(tmp[b % 2][:, h * P:(h + 1) * P],
                                           ps[2 - b // 2 % 2][:, b % 2, h * P:(h + 1) * P],
                                           ACT.Copy, scale=kw_s[:, h, b:b + 1])
                        if h < NH - 1:
                            own.mark(r)
                    r.then_inc(vkw_ready.sem, 1)
                act.wait_ge(*num_done.at(l, 1))
                act.activation(den_s[:].rearrange("p a b -> p (a b)"), ps[3][:, 1, 0:NH * NS], ACT.Abs)\
                    .then_inc(dens_abs.sem, 1)
                act.wait_ge(*hs_ready.at(l, 1))
                act.activation(tmp[3][:, 0:NH * NS].rearrange("p (a b) -> p a b", a=NH), q[:, :, TP:T], ACT.Square)\
                    .then_inc(h_square.sem, 1)
                act.wait_ge(*h_summed.at(l, 1))
                act.activation(den_s[:].rearrange("p a b -> p (a b)"), ps[3][:, 1, 0:NH * NS], ACT.Sqrt, bias=EPS,
                               scale=1.0 / P).then_inc(h_root.sem, 1)
                act.activation(cat_h[:, 0:2, :], gv[:], ACT.Copy).then_inc(cat_hi.sem, 1)
                act.activation(cat_h[:, 6:8, :], gu[:], ACT.Copy).then_inc(cat_hi.sem, 1)
                hi(l, TURNS["branch"], 1, FULL)
                act.wait_ge(*h_ready.at(l, 1))
                act.activation(cat_h[:, 2:6, :], q[:], ACT.Copy).then_inc(cat_hi.sem, 1)

            def branches(l):
                def evict(i, s):
                    for u in range(2):
                        g = 2 * s + u
                        act.wait_ge(*done("branch", l, i * 4 + (g + 1)))
                        if g < 3:
                            act.wait_ge(*branch_read.at(l, i * 5))
                            act.activation(two(tmp[g][:]), ps[g][:, :, 0:HT], ACT.Sigmoid)\
                                .then_inc(gate_ready.sem, 1)
                        else:
                            act.wait_ge(*branch_read.at(l, i * 5 + 5))
                            m = bass.ds(i, 1) if not isinstance(i, int) else slice(i, i + 1)
                            act.activation(mrg_h[:, m, :], tmp[3][:].unsqueeze(1), ACT.Copy).then_inc(mrg_hi.sem, 1)

                stream(l, "branch", 8, FULL, evict, FULL, True)

            def memory_hi(l):
                act.wait_ge(*mem_scaled.at(l, 1))
                for g in range(2):
                    r = slice(4 * g, 4 * g + 4)
                    act.activation(mem_h[:, r, :], mem[:, r, :], ACT.Copy).then_inc(mem_hi.sem, 1)

            def memory(l):
                def hi_kv(p):
                    hi(l, TURNS["mk"] + p // 2, p % 2, FULL)

                def evict_kv(p):
                    for u in range(2):
                        act.wait_ge(*done("mk", l, 2 * p + u + 1))
                        dst, m = (mk, mvT)[p // 4], 2 * (p % 4) + u
                        r = act.activation(dst[:, m, :], ps[p % 2][:, u, 0:M], ACT.Copy)
                    r.then_inc(pair_evicted[p % 2].sem, 1)

                hi_kv(1)
                post(l, 1)
                evict_kv(0)
                hi_kv(2)
                evict_kv(1)
                pre_squares(l, PRE_ATT, 2, range(0, 6))
                hi_kv(3)
                pre_squares(l, PRE_ATT, 2, range(6, 8))
                pre_root(l, PRE_ATT)
                evict_kv(2)
                hi_kv(4)
                evict_kv(3)
                hi_kv(5)
                pre_hi(l, PRE_ATT, range(0, 2))
                evict_kv(4)
                hi_kv(6)
                pre_hi(l, PRE_ATT, range(2, 5))
                evict_kv(5)
                hi_kv(7)
                pre_hi(l, PRE_ATT, range(5, 8))
                evict_kv(6)
                hi_kv(8)
                evict_kv(7)

                def evict_q(i, s):
                    for u in range(2):
                        act.wait_ge(*done("mq", l, i * 4 + (2 * s + u + 1)))
                        n = i * 4 + (2 * s + u)
                        dst = qm[:, n, :] if isinstance(i, int) else \
                            qm[:, bass.ds(n, 1), :].rearrange("p a t -> p (a t)")
                        r = act.activation(two(dst), ps[2 * s + u][:, :, 0:HT], ACT.Copy, scale=float(M) ** -0.5)
                    r.then_inc(pair_evicted[s].sem, 1)

                stream(l, "mq", 2, FULL, evict_q, FULL)

            def attention(l):
                def exps(h):
                    act.wait_ge(*max_ready.at(l, h + 1))
                    act.wait_ge(*(pT_done.at(l, h) if h else mvT_done.at(l, 1)))
                    for t in range(NC):
                        r = act.activation(prob[:, t, :], ps[h % 2][:, t // 2, (t % 2) * M:(t % 2 + 1) * M],
                                           ACT.Exp, bias=att_max[:, h % 2, t:t + 1], accum_out=att_sum[:, t:t + 1])
                        if t < NC - 1:
                            own.mark(r)
                    r.then_inc(p_ready.sem, 1)

                def transposed(h):
                    act.wait_ge(*pT_done.at(l, h + 1))
                    act.activation(probT[:], ps[2][:], ACT.Copy).then_inc(pT_ready.sem, 1)

                def output(h):
                    act.wait_ge(*o_done.at(l, h + 1))
                    act.activation(xh[:, 2 * h:2 * h + 2, 0:TP], ps[h % 2][:], ACT.Copy).then_inc(oh_ready.sem, 1)

                exps(0)
                for h in range(NH):
                    transposed(h)
                    if h == NH - 1:
                        act.wait_ge(*smax_ready.at(l, 1))
                        for g in range(NH):
                            r = act.activation(prob_s[:, g, :], ps[3][0:NS, g // 2, (g % 2) * M:(g % 2 + 1) * M],
                                               ACT.Exp, bias=att_smax[:, g:g + 1], accum_out=att_ssum[:, g:g + 1])
                            if g < NH - 1:
                                own.mark(r)
                        r.then_inc(sexp_ready.sem, 1)
                    if h + 1 < NH:
                        exps(h + 1)
                    output(h)
                act.wait_ge(*v_used.at(l, NS))
                act.activation(o_rows[:].rearrange("p (a b) -> p a b", a=2), ps[3][0:NS, :, :], ACT.Copy)\
                    .then_inc(orow_ready.sem, 1)
                act.wait_ge(*oT_done.at(l, 1))
                act.activation(xh[:, :, TP:T], ps[2][:, 0, 0:64].rearrange("p (a b) -> p a b", a=KD), ACT.Copy)\
                    .then_inc(oh_ready.sem, 1)

            act.wait_ge(mem_first.sem, 32)
            act.activation(mem[:], mem[:], ACT.Square).then_inc(mem_square.sem, 1)
            act.wait_ge(mem_summed.sem, 1)
            act.activation(mem_rms[:], ps[2][:, 0, 0:M], ACT.Sqrt, bias=EPS, scale=1.0 / D).then_inc(mem_root.sem, 1)
            with act.Fori(0, L) as l:
                own.begin(l)
                hi(l, TURNS["up_a"], 0, FULL)
                pre(l, PRE_A, 0)
                ffn(l, 0, "up_a", "down_a", FULL)
                post(l, 0)
                pre(l, PRE_MIX, 1)
                evict = evict_in(l)
                for i in range(6):
                    hi(l, TURNS["in"] + i, 1, FULL)
                    if i == 0:
                        softplus(l)
                    evict(i, 0)
                    hi(l, TURNS["in"] + i + 1, 0, FULL)
                    evict(i, 1)
                    if i == 2:
                        gate_exps(l)
                mixer(l)
                branches(l)
                stream(l, "out", 2, FULL, squares(l, 1, "out"), FULL, between=memory_hi)
                memory(l)
                attention(l)
                stream(l, "mo", 2, FULL, squares(l, 2, "mo"), FULL)
                post(l, 2)
                pre(l, PRE_B, 3)
                act.wait_ge(out_mem.sem, l * 32 + 32)
                ffn(l, 1, "up_b", "down_b", None)
                post(l, 3)
                own.end("scalar")

        @block.vector
        def _(dve):
            own = Steps(dve, vector_step)
            dve.memset(zeros8[:], 0.0).then_inc(zeros_ready.sem, 1)
            dve.sem_inc(pair_evicted[0].sem, 1)
            dve.sem_inc(pair_evicted[1].sem, 1)
            dve.sem_inc(hidden_lo.sem, hidden_lo.credit)
            dve.sem_inc(x_even.sem, x_even.credit)
            dve.sem_inc(x_odd.sem, x_odd.credit)
            dve.sem_inc(y_summed.sem, y_summed.credit)
            dve.sem_inc(branch_read.sem, branch_read.credit)
            dve.wait_ge(s_x.sem, 7 * 16)
            dve.wait_ge(mem_root.sem, 1)
            dve.reciprocal(mem_rms[:], mem_rms[:]).then_inc(mem_inverse.sem, 1)
            for n, g in enumerate((gain(0, 1), gain(3, 1))):
                dve.tensor_scalar(vec_all[:, :, g:g + KD], vec_all[:, :, g:g + KD], 0.5, None, ALU.mult)\
                    .then_inc(const_scaled.sem, 1)
            dve.wait_ge(const_scaled.sem, 2)

            def start_sum(l, group):
                dve.memset(ssq[:], 0.0).then_inc(y_summed.sem, 1)

            def evict_y(l, group, units_at, m, tile):
                dve.wait_ge(*y_square.at(l, m + (group * KD + 1)))
                dve.wait_ge(*y_summed.at(l, m + (group * (KD + 1) + 1)))
                dve.tensor_tensor(ssq[:], ssq[:], tmp[tile % 2 if units_at else tile // 2][:], ALU.add)\
                    .then_inc(y_summed.sem, 1)
                dst = y[:, m, :] if isinstance(m, int) else y[:, bass.ds(m, 1), :].rearrange("p a t -> p (a t)")
                return dve.tensor_copy(two(dst), ps[tile][:, :, 0:HT])

            def linear_y(l, group, phase):
                if phase == "out":
                    dve.wait_ge(out_mix.sem, l * 144 + 144)
                start_sum(l, group)

                def turn(i):
                    for s in range(2):
                        for u in range(2):
                            r = evict_y(l, group, True, i * 4 + (2 * s + u), 2 * s + u)
                        r.then_inc(pair_evicted[s].sem, 1)

                if phase == "out":
                    memory_scale(l)
                    turn(0)
                    memory_lo(l)
                    turn(1)
                else:
                    with dve.Fori(0, 2) as i:
                        turn(i)

            def memory_scale(l):
                dve.wait_ge(mem_loaded.sem, l * 16 + 16)
                dve.wait_ge(mem_inverse.sem, 1)
                for m in range(KD):
                    ins = dve.scalar_tensor_tensor(out=mem[:, m, :], in0=mem[:, m, :],
                                                   scalar=vec[:, V_MEM + m:V_MEM + m + 1], in1=mem_rms[:],
                                                   op0=ALU.mult, op1=ALU.mult)
                    if m < KD - 1:
                        own.mark(ins)
                ins.then_inc(mem_scaled.sem, 1)

            def memory_lo(l):
                for g in range(2):
                    r = slice(4 * g, 4 * g + 4)
                    dve.wait_ge(*mem_hi.at(l, g + 1))
                    dve.tensor_tensor(mem_l[:, r, :], mem[:, r, :], mem_h[:, r, :].bitcast(F32), ALU.subtract)\
                        .then_inc(mem_lo.sem, 1)

            def ffn(l, n, up, down):
                with dve.Fori(0, 11) as i:
                    for s in range(2):
                        f = i * 2 + s
                        at = f + n * KF
                        dve.wait_ge(*silu_ready.at(l, at + 1))
                        dve.wait_ge(*done(up, l, i * 4 + (2 * s + 2)))
                        dve.wait_ge(*hidden_lo.at(l, at - 1))
                        dve.tensor_tensor(two(tmp[2 + s][:]), two(tmp[s][:]), ps[2 * s + 1][:, :, 0:HT], ALU.mult)\
                            .then_inc(pair_evicted[s].sem, 1)
                        dve.wait_ge(*hidden_hi.at(l, at + 1))
                        dve.tensor_tensor(hid_l[:, bass.ds(f, 1), :], tmp[2 + s][:].unsqueeze(1),
                                          hid_h[:, bass.ds(f, 1), :].bitcast(F32), ALU.subtract)\
                            .then_inc(hidden_lo.sem, 1)
                start_sum(l, 3 * n)
                with dve.Fori(0, 4) as i:
                    for mm in range(2):
                        evict_y(l, 3 * n, False, i * 2 + mm, 2 * mm).then_inc(pair_evicted[mm].sem, 1)

            def post(l, n, g):
                dve.wait_ge(*root_ready.at(l, ROOT_POST[n] + 1))
                own.link(dve.reciprocal(rms[:], rms[:]))

                def scaled(m):
                    if m >= 2:
                        dve.wait_ge(*x_updated(l, n, m - 2))
                    ins = dve.scalar_tensor_tensor(out=tmp[m % 2][:], in0=y[:, m, :], scalar=vec[:, g + m:g + m + 1],
                                                   in1=rms[:], op0=ALU.mult, op1=ALU.mult)
                    if m % 2 and n != 1:
                        ins.then_inc(y_scaled.sem, 1)
                    else:
                        own.mark(ins)
                    return own.n

                nxt = scaled(0)
                for m in range(KD):
                    mine = nxt
                    if m + 1 < KD:
                        nxt = scaled(m + 1)
                    if m % 2 == 0 or n == 1:
                        dve.wait_ge(*vector_step.at(l, mine))
                        dve.tensor_tensor(x[:, m, :], x[:, m, :], tmp[m % 2][:], ALU.add)\
                            .then_inc((x_even, x_odd)[m % 2].sem, 1)

            def pre(l, n, g):
                dve.wait_ge(*root_ready.at(l, ROOT_PRE[n] + 1))
                own.link(dve.reciprocal(rms[:], rms[:]))

                def normal(m):
                    if m >= 2:
                        dve.wait_ge(*xl_ready(l, n, m - 2))
                    dve.scalar_tensor_tensor(out=tmp[m % 2][:], in0=x[:, m, :], scalar=vec[:, g + m:g + m + 1],
                                             in1=rms[:], op0=ALU.mult, op1=ALU.mult).then_inc(xn_ready.sem, 1)

                normal(0)
                for m in range(KD):
                    if m + 1 < KD:
                        normal(m + 1)
                    if m % 2 == 0 or n == PRE_ATT:
                        dve.wait_ge(*xh_ready.at(l, n * KD + m + 1))
                        dve.tensor_tensor(xl[:, m, :], tmp[m % 2][:], xh[:, m, :].bitcast(F32), ALU.subtract)\
                            .then_inc((xl_even, xl_odd)[m % 2].sem, 1)

            def gates_rows(l):
                dve.wait_ge(*done("in", l, 1))
                own.mark(dve.tensor_scalar(two(tmp[0][0:NH, :]), ps[0][0:NH, :, 0:HT], vec[0:NH, V_BI:V_BI + 1],
                                           None, ALU.add))
                dve.wait_ge(*done("in", l, 2))
                dve.tensor_scalar(two(tmp[1][0:NH, :]), ps[1][0:NH, :, 0:HT], vec[0:NH, V_BF:V_BF + 1],
                                  None, ALU.add).then_inc(pair_evicted[0].sem, 1)

            def mixer(l):
                ig, lf, sp_, mt = (tmp[n][0:NH, :] for n in range(4))
                one, a, g = ssq[0:NH, 0:TP], rms[0:NH, 0:TP], ssq[0:NH, 0:TP]
                dve.memset(pin[:, :, 0:PAD], 0.0).then_inc(win_zero.sem, 1)
                gates_rows(l)
                own.mark(dve.memset(one, 1.0))
                dve.wait_ge(*softplus_ready.at(l, 1))
                own.link(dve.scalar_tensor_tensor(out=lf, in0=lf, scalar=0.0, in1=sp_, op0=ALU.min, op1=ALU.subtract))
                own.link(dve.tensor_tensor_scan(mt[:, 0:TP], one, lf[:, 0:TP], 0.0, ALU.mult, ALU.add))
                own.link(dve.tensor_tensor(a, ig[:, 0:TP], mt[:, 0:TP], ALU.subtract))
                own.link(dve.tensor_tensor_scan(g, a, a, 0.0, ALU.max, ALU.max))
                dve.tensor_tensor(mt[:, 0:TP], mt[:, 0:TP], g, ALU.add).then_inc(mt_ready.sem, 1)
                own.link(dve.tensor_scalar(rows[:, 0:TP], g, -1.0, None, ALU.mult))
                own.mark(dve.tensor_copy(m_last[:], mt[:, TP - 1:TP]))
                dve.wait_ge(mix_loaded.sem, l * 96 + 96)
                own.mark(dve.tensor_copy(pool_new[:, :, :, 0:14], pool_state[:, :, :, 1:15]))
                own.link(dve.tensor_tensor(m_args[:, 0, :], lf[:, TP:T], m_state[:], ALU.add))
                own.link(dve.tensor_tensor(m_new[:], m_args[:, 0, :], ig[:, TP:T], ALU.max))
                own.mark(dve.tensor_tensor(m_args[:, 0, :], m_args[:, 0, :], m_new[:], ALU.subtract))
                own.mark(dve.tensor_tensor(m_args[:, 1, :], ig[:, TP:T], m_new[:], ALU.subtract))
                dve.tensor_scalar(m_args[:, 2, :], m_new[:], -1.0, None, ALU.mult).then_inc(args_ready.sem, 1)
                dve.tensor_scalar(lf[:, 0:TP], a, rows[:, TP - 1:TP], None, ALU.add).then_inc(args_ready.sem, 1)
                dve.wait_ge(*evicted("in", 1, l, 1))
                own.mark(dve.tensor_copy(pool_last[:], pin[:, :, PAD + TP - 15:PAD + TP]))
                own.mark(dve.tensor_copy(pool_new[:, :, :, 14:15], pin[:, :, PAD + TP:].unsqueeze(3)))
                dve.wait_ge(*win_ready.at(l, 4))
                groups = ((2, 0, 0, winA), (4, 0, 64, winB), (8, 1, 0, winA), (16, 1, 64, winB))
                for w, j, p0, win in groups:
                    r = slice(p0, p0 + 64)
                    own.mark(dve.tensor_tensor(win[r, j, PAD:2 * PAD], win[r, j, PAD:2 * PAD], early[r, j, :], ALU.mult))
                    own.mark(dve.tensor_reduce(pool_red[r, j, :], pool_state[r, j, :, 16 - w:15], AX.X, ALU.add))
                own.settle()
                for w, j, p0, win in groups:
                    r = slice(p0, p0 + 64)
                    own.mark(dve.scalar_tensor_tensor(out=winA[r, j, PAD:PAD + TP], in0=win[r, j, PAD:PAD + TP],
                                                      scalar=1.0 / w, in1=pin[r, j, PAD:PAD + TP],
                                                      op0=ALU.mult, op1=ALU.subtract))
                    own.mark(dve.tensor_tensor(pool_red[r, j, :], pool_red[r, j, :], pin[r, j, PAD + TP:], ALU.add))
                own.settle()
                for n, (w, j, p0, win) in enumerate(groups):
                    r = slice(p0, p0 + 64)
                    ins = dve.scalar_tensor_tensor(out=winA[r, j, PAD + TP:], in0=pool_red[r, j, :], scalar=1.0 / w,
                                                   in1=pin[r, j, PAD + TP:], op0=ALU.mult, op1=ALU.subtract)
                    if n < 3:
                        own.mark(ins)
                ins.then_inc(diff_ready.sem, 1)
                dve.wait_ge(*mean_done.at(l, 1))
                own.mark(dve.scalar_tensor_tensor(out=two(gv[:, 0, :]), in0=ps[2][:, :, 0:HT], scalar=-1.0 / 256,
                                                  in1=two(gv[:, 0, :]), op0=ALU.mult, op1=ALU.add))
                dve.wait_ge(*exps_ready.at(l, 3))
                dve.scalar_tensor_tensor(out=two(gv[:, 1, :]), in0=ps[2][:, :, 0:HT], scalar=-1.0 / 256,
                                         in1=two(gv[:, 1, :]), op0=ALU.mult, op1=ALU.add).then_inc(centered.sem, 1)
                dve.wait_ge(*cols_done.at(l, 1))
                dve.tensor_copy(cols[:].rearrange("p a b c -> p (a b c)"), ps[3][:, 0, 0:48])\
                    .then_inc(cols_ready.sem, 1)
                dve.tensor_copy(s_rows[:].rearrange("p a b c -> p (a b c)"), ps[3][:, 1, 0:96])\
                    .then_inc(cols_ready.sem, 1)
                for t in range(2):
                    dve.wait_ge(*tok_done.at(l, 3 + t))
                    dve.tensor_copy(v_tok[:, 2 * t:2 * t + 2, :, 0:P],
                                    ps[t][:].rearrange("p a (b c) -> p a b c", b=NC)).then_inc(vtok_ready.sem, 1)
                dve.memset(v_tok[:, :, :, P:P + 1], 1.0).then_inc(vones_ready.sem, 1)
                dve.wait_ge(*var_root.at(l, 1))
                own.link(dve.reciprocal(tmp[2][:], tmp[2][:]))
                for j in range(2):
                    own.mark(dve.scalar_tensor_tensor(out=gv[:, j, :], in0=gv[:, j, :],
                                                      scalar=vec[:, V_LNG + j:V_LNG + j + 1], in1=tmp[2][:],
                                                      op0=ALU.mult, op1=ALU.mult))
                own.settle()
                for j in range(2):
                    own.mark(dve.tensor_scalar(gv[:, j, :], gv[:, j, :], vec[:, V_LNB + j:V_LNB + j + 1], None, ALU.add))
                own.settle()
                dve.tensor_copy(gv_out[:], gv[:, :, TP:T]).then_inc(vn_ready.sem, 1)
                dve.wait_ge(*mixed_done.at(l, 1))
                for j in range(2):
                    own.mark(dve.tensor_tensor(tmp[j][:, 0:TP].rearrange("p (c t) -> p c t", c=NC),
                                               ps[3][:, j, :].rearrange("p (c t) -> p c t", c=NC),
                                               bs_m[:, j:j + 1, :].to_broadcast([P, NC, P]), ALU.add))
                    own.mark(dve.tensor_scalar(tmp[j][:, TP:T], gv[:, j, TP:T], vec[:, V_WS0 + j:V_WS0 + j + 1],
                                               vec[:, V_BS0 + j:V_BS0 + j + 1], ALU.mult, ALU.add))
                own.settle()
                own.mark(dve.tensor_tensor(gu[:, 0, :], gu[:, 0, :], tmp[0][:], ALU.mult))
                dve.tensor_tensor(gu[:, 1, :], gu[:, 1, :], tmp[1][:], ALU.mult).then_inc(gmlp_ready.sem, 1)
                own.link(dve.tensor_tensor(kw_s[:], k[:, :, TP:T], s_rows[:, :, 1, :], ALU.mult))
                own.link(dve.tensor_tensor(n_state[:], n_state[:], s_rows[:, :, 0, :], ALU.mult))
                own.link(dve.tensor_tensor(n_state[:], n_state[:], kw_s[:], ALU.add))
                dve.tensor_tensor(qn_s[:], n_state[:], q[:, :, TP:T], ALU.mult).then_inc(qn_ready.sem, 1)
                dve.wait_ge(*gb_ready.at(l, 2))
                dve.wait_ge(*pooled.at(l, 1))

                def exponents(h):
                    if h >= 2:
                        dve.wait_ge(*head_sums.at(l, h - 1))
                    sw_, at = sws[h % 2], 0
                    for j in range(NC):
                        n = TP - j * P
                        col = cols[:, 0, j, h:h + 1]
                        d = dve.scalar_tensor_tensor(out=sw_[:, at:at + P], in0=v[:, h, j * P:(j + 1) * P],
                                                     scalar=col, in1=neg_mask[:], op0=ALU.add, op1=ALU.min)
                        if n > P:
                            own.mark(d)
                            d = dve.tensor_scalar(sw_[:, at + P:at + n], v[:, h, (j + 1) * P:TP], col, 0.0,
                                                  ALU.add, ALU.min)
                        d.then_inc(d_ready.sem, 1)
                        at += n

                exponents(0)
                for h in range(NH):
                    dve.wait_ge(*head_scores.at(l, h + 1))
                    sw_, at = sws[h % 2], 0
                    for j in range(NC):
                        n = TP - j * P
                        dve.wait_ge(*w_ready.at(l, h * NC + j + 1))
                        dve.tensor_tensor(sw_[:, at:at + n], sw_[:, at:at + n], score(h, j), ALU.mult)\
                            .then_inc(sw_ready.sem, 1)
                        at += n
                    if h + 1 < NH:
                        exponents(h + 1)
                dve.wait_ge(*head_read.at(l, NH))
                den = h_tok[:, :, :, P:P + 1].rearrange("p h j a -> p h (j a)")
                own.link(dve.scalar_tensor_tensor(out=h_den[:], in0=den, scalar=-1.0,
                                                  in1=cols[:, 2, :, :].rearrange("p j h -> p h j"),
                                                  op0=ALU.mult, op1=ALU.max))
                own.link(dve.tensor_tensor(h_den[:], h_den[:], den, ALU.max))
                own.link(dve.reciprocal(h_den[:], h_den[:]))
                own.link(dve.tensor_tensor(h_rms[:], h_sum[:], h_den[:], ALU.mult))
                dve.tensor_tensor(h_rms[:], h_rms[:], h_den[:], ALU.mult).then_inc(h_mean.sem, 1)
                dve.wait_ge(*h_rooted.at(l, 1))
                own.link(dve.reciprocal(h_rms[:], h_rms[:]))
                own.link(dve.tensor_tensor(h_rms[:], h_rms[:], h_den[:], ALU.mult))
                dve.tensor_tensor(h_tok[:, :, :, 0:P], h_tok[:, :, :, 0:P],
                                  h_rms[:].unsqueeze(3).to_broadcast([P, NH, NC, P]), ALU.mult)\
                    .then_inc(htok_ready.sem, 1)
                dve.wait_ge(*hT_done.at(l, 1))
                for h in range(NH):
                    ins = dve.scalar_tensor_tensor(out=q[:, h, 0:TP], in0=ps[h // 2][:, h % 2, :],
                                                   scalar=vec[:, V_MLSTM + h:V_MLSTM + h + 1], in1=og[:, h, 0:TP],
                                                   op0=ALU.mult, op1=ALU.mult)
                    if h < NH - 1:
                        own.mark(ins)
                ins.then_inc(hT_read.sem, 1)
                dve.wait_ge(*Cw_ready.at(l, 1))
                for b in range(NS):
                    dve.wait_ge(*vkw_ready.at(l, b + 1))
                    dve.tensor_tensor(C_s[:, b, :, :], C_s[:, b, :, :],
                                      tmp[b % 2][:, 0:TP].rearrange("p (a b) -> p a b", a=NH), ALU.add)\
                        .then_inc(Cs_ready.sem, 1)
                dve.wait_ge(*dens_abs.at(l, 1))
                own.link(dve.tensor_tensor(den_s[:], den_s[:], s_rows[:, :, 2, :], ALU.max))
                own.link(dve.reciprocal(den_s[:], den_s[:]))
                dve.tensor_tensor(q[:, :, TP:T], ps[3][:, 0, 0:NH * NS].rearrange("p (a b) -> p a b", a=NH), den_s[:],
                                  ALU.mult).then_inc(hs_ready.sem, 1)
                dve.wait_ge(*h_root.at(l, 1))
                own.link(dve.reciprocal(den_s[:], den_s[:]))
                own.link(dve.tensor_tensor(q[:, :, TP:T], q[:, :, TP:T], den_s[:], ALU.mult))
                for h in range(NH):
                    ins = dve.scalar_tensor_tensor(out=q[:, h, TP:T], in0=q[:, h, TP:T],
                                                   scalar=vec[:, V_MLSTM + h:V_MLSTM + h + 1], in1=og[:, h, TP:T],
                                                   op0=ALU.mult, op1=ALU.mult)
                    if h < NH - 1:
                        own.mark(ins)
                ins.then_inc(h_ready.sem, 1)
                for n, (lo_, hi_, src) in enumerate(((0, 2, gv), (6, 8, gu), (2, 6, q))):
                    dve.wait_ge(*cat_hi.at(l, n + 1))
                    dve.tensor_tensor(cat_l[:, lo_:hi_, :], src[:], cat_h[:, lo_:hi_, :].bitcast(F32), ALU.subtract)\
                        .then_inc(cat_lo.sem, 1)

            def branches(l):
                with dve.Fori(0, KD) as m:
                    for n in range(2):
                        dve.wait_ge(*gate_ready.at(l, m * 3 + (2 + n)))
                        dve.wait_ge(*branch_done.at(l, m * 2 + (n + 1)))
                        dve.tensor_tensor(two(tmp[1 + n][:]), two(tmp[1 + n][:]), ps[n][:, :, 0:HT], ALU.mult)\
                            .then_inc(branch_read.sem, 1)
                    dve.wait_ge(*done("branch", l, m * 4 + 4))
                    dve.tensor_tensor(two(tmp[0][:]), two(tmp[0][:]), ps[3][:, :, 0:HT], ALU.mult)\
                        .then_inc(branch_read.sem, 1)
                    dve.wait_ge(*branch_read.at(l, m * 5 + 3))
                    dve.tensor_tensor(tmp[1][:], tmp[1][:], tmp[2][:], ALU.add).then_inc(branch_read.sem, 1)
                    dve.wait_ge(*branch_read.at(l, m * 5 + 4))
                    dve.tensor_tensor(tmp[3][:], tmp[0][:], tmp[1][:], ALU.add).then_inc(branch_read.sem, 1)
                    dve.wait_ge(*mrg_hi.at(l, m + 1))
                    dve.tensor_tensor(mrg_l[:, bass.ds(m, 1), :], tmp[3][:].unsqueeze(1),
                                      mrg_h[:, bass.ds(m, 1), :].bitcast(F32), ALU.subtract).then_inc(mrg_lo.sem, 1)

            def attention(l):
                def maxima(h):
                    dve.wait_ge(*sc_done.at(l, h + 1))
                    dve.tensor_reduce(att_max[:, h % 2, :], ps[h % 2][:].rearrange("p b (t m) -> p (b t) m", t=2),
                                      AX.X, ALU.max, negate=True).then_inc(max_ready.sem, 1)

                def probs(h):
                    dve.wait_ge(*p_ready.at(l, h + 1))
                    own.link(dve.reciprocal(att_sum[:], att_sum[:]))
                    for t in range(NC):
                        ins = dve.tensor_scalar(prob[:, t, :], prob[:, t, :], att_sum[:, t:t + 1], None, ALU.mult)
                        if t < NC - 1:
                            own.mark(ins)
                    ins.then_inc(pn_ready.sem, 1)

                def lo_out(h):
                    dve.wait_ge(*oh_ready.at(l, h + 1))
                    dve.tensor_tensor(xl[:, 2 * h:2 * h + 2, 0:TP], ps[h % 2][:],
                                      xh[:, 2 * h:2 * h + 2, 0:TP].bitcast(F32), ALU.subtract)\
                        .then_inc(ol_ready.sem, 1)

                every = [P, KD, NS, NS]
                for s in range(2):
                    dve.wait_ge(*evicted("mq", s, l, 2))
                dve.tensor_tensor(q_one[:], qm[:, :, TP:T].unsqueeze(2).to_broadcast(every),
                                  eye8[:].unsqueeze(1).to_broadcast(every), ALU.mult).then_inc(q_one_ready.sem, 1)
                maxima(0)
                dve.wait_ge(*mvT_done.at(l, 1))
                for mt in range(2):
                    ins = dve.tensor_copy(mv[:, mt, :].rearrange("p (b n) -> p b n", b=2), ps[2 + mt][:])
                    if mt == 0:
                        own.mark(ins)
                ins.then_inc(mv_ready.sem, 1)
                maxima(1)
                probs(0)
                probs(1)
                for h in range(2):
                    lo_out(h)
                    maxima(h + 2)
                    probs(h + 2)
                lo_out(2)
                dve.wait_ge(*k_used.at(l, NS))
                dve.tensor_reduce(att_smax[:], ps[3][0:NS].rearrange("p b (t m) -> p (b t) m", t=2), AX.X, ALU.max,
                                  negate=True).then_inc(smax_ready.sem, 1)
                dve.wait_ge(*sexp_ready.at(l, 1))
                own.link(dve.reciprocal(att_ssum[:], att_ssum[:]))
                for h in range(NH):
                    ins = dve.tensor_scalar(prob_s[:, h, :], prob_s[:, h, :], att_ssum[:, h:h + 1], None, ALU.mult)
                    if h < NH - 1:
                        own.mark(ins)
                ins.then_inc(sp_ready.sem, 1)
                dve.wait_ge(*spT_done.at(l, 1))
                dve.tensor_tensor(p_one[:], ps[3][:, 0, 0:KD * NS].rearrange("p (f s) -> p f s", f=KD).unsqueeze(2)
                                  .to_broadcast(every), eye8[:].unsqueeze(1).to_broadcast(every), ALU.mult)\
                    .then_inc(spT_ready.sem, 1)
                lo_out(3)
                dve.wait_ge(*oh_ready.at(l, NH + 1))
                dve.tensor_tensor(xl[:, :, TP:T], ps[2][:, 0, 0:64].rearrange("p (a b) -> p a b", a=KD),
                                  xh[:, :, TP:T].bitcast(F32), ALU.subtract).then_inc(ol_ready.sem, 1)

            with dve.Fori(0, L) as l:
                own.begin(l)
                dve.wait_ge(*x_updated(l, -1, KD - 1))
                dve.tensor_copy(vec[:], vec_all[:, bass.ds(l, 1), :].rearrange("p a n -> p (a n)"))\
                    .then_inc(vec_ready.sem, 1)
                dve.wait_ge(*vec_ready.at(l, 1))
                pre(l, PRE_A, gain(0, 0))
                ffn(l, 0, "up_a", "down_a")
                post(l, 0, gain(0, 1))
                pre(l, PRE_MIX, gain(1, 0))
                mixer(l)
                branches(l)
                linear_y(l, 1, "out")
                post(l, 1, gain(1, 1))
                pre(l, PRE_ATT, gain(2, 0))
                attention(l)
                linear_y(l, 2, "mo")
                post(l, 2, gain(2, 1))
                pre(l, PRE_B, gain(3, 0))
                ffn(l, 1, "up_b", "down_b")
                post(l, 3, gain(3, 1))
                own.end("vector")


def _layout(inp):
    f = np.float32
    cut = np.ascontiguousarray
    a = {k: np.asarray(v) for k, v in inp.items()}

    def tiles(w):
        K, N = w.shape
        return w.reshape(K // P, P, N // P, P).transpose(2, 1, 0, 3)

    def cols(w):
        return w.reshape(-1, P).T

    x = np.concatenate([a["x_prompt"][0], a["x_sample"][:, 0]], axis=0)
    out = {"xT": cut(x.T.reshape(KD, P, T).transpose(1, 0, 2)),
           "memT": cut(a["mem_prompt"][0].T.reshape(KD, P, M).transpose(1, 0, 2))}
    full, down, vecs = [], [], []
    for l in range(L):
        w_in = a["w_in"][l]
        up = [tiles(a["w_ff_in"][l, n]) for n in range(2)]
        ups = [np.stack([u[:KF], u[KF:]], axis=1).reshape(2 * KF, P, KD, P) for u in up]
        first = tiles(w_in[:, :2304])
        i_f = np.stack([w_in[:, c:c + P].reshape(KD, P, P).transpose(1, 0, 2) for c in (2304, 2308)])
        ugv = tiles(w_in[:, 2312:2824])
        gates = tiles(w_in[:, 2824:]).reshape(3, KD, P, KD, P)
        br = tiles(np.concatenate([a["w_br_pool"][l], a["w_br_mlstm"][l], a["w_br_gmlp"][l]], axis=0))
        branch = np.stack([gates[0], gates[1], gates[2], br], axis=1).reshape(4 * KD, P, KD, P)
        units = [ups[0], i_f, first[:2], ugv, first[14:], first[2:14], branch] + [tiles(a[n][l]) for n in ("w_out", "w_mk", "w_mv", "w_mq", "w_mo")]
        units = np.concatenate(units + [ups[1]], axis=0)
        full.append(units.reshape(FULL_PAIRS, 2, P, KD * P).transpose(0, 2, 1, 3).reshape(FULL_PAIRS, P, 2 * KD * P))
        for n in range(2):
            w = tiles(a["w_ff_out"][l, n])
            down.append(w.reshape(KD, P, 2, 11 * P).transpose(0, 2, 1, 3).reshape(2 * KD, P, 11 * P))
        ws0, bs0 = a["w_s"][l, :, 0, 0], a["b_s"][l, :, 0]
        b_i, b_f = np.zeros((P, 1), f), np.zeros((P, 1), f)
        b_i[:NH, 0], b_f[:NH, 0] = a["b_igate"][l], a["b_fgate"][l]
        vecs.append(np.concatenate(
            [cols(a["norm_g"][l].reshape(-1)), cols(a["g_mem"][l]), cols(a["g_mlstm"][l]), cols(a["gmlp_ln_g"][l]),
             cols(a["gmlp_ln_b"][l]), cols(a["s_pool"][l]), cols(np.repeat(ws0, 64)), cols(np.repeat(bs0, 64)),
             b_i, b_f], axis=1))
    out["w_full"] = cut(np.concatenate(full, axis=0))
    out["w_down"] = cut(np.concatenate(down, axis=0))
    out["vecs"] = cut(np.stack(vecs, axis=1))
    wp = np.zeros((L, P, 2, P), f)
    for g in range(4):
        r = slice(64 * (g % 2), 64 * (g % 2) + 64)
        wp[:, r, g // 2, r] = a["w_pool"][:, g]
    out["wpool"] = wp.reshape(L, P, 2 * P)
    out["wsT"] = cut(a["w_s"].transpose(0, 3, 1, 2).reshape(L, P, 4 * P))
    out["bsT"] = cut(np.repeat(a["b_s"].reshape(L, 2, 2, 1, P), 64, axis=3).transpose(0, 2, 3, 1, 4).reshape(L, P, 2 * P))
    out["poolT"] = cut(a["state_pool"].transpose(0, 3, 1, 2).reshape(L, 2, P, NS * 15).transpose(0, 2, 1, 3)
                       .reshape(L, P, 2 * NS * 15))
    out["CT"] = cut(a["state_mlstm_C"].transpose(0, 4, 1, 2, 3).reshape(L, P, NS * NH * P))
    out["nT"] = cut(a["state_mlstm_n"].transpose(0, 3, 2, 1).reshape(L, P, NH * NS))
    out["mT"] = cut(a["state_mlstm_m"].transpose(0, 2, 1))
    out["kT"] = cut(a["cache_mem_k"].transpose(0, 1, 3, 4, 2).reshape(L * NS, KD, P, M).transpose(0, 2, 1, 3)
                    .reshape(L * NS, P, KD * M))
    out["vC"] = cut(a["cache_mem_v"].reshape(L * NS, 2, P, D).transpose(0, 2, 1, 3).reshape(L * NS, P, 2 * D))
    s, t = np.arange(P)[:, None], np.arange(P)[None, :]
    window = np.repeat(np.array([[2, 8], [4, 16]]), 64, axis=0)[:, :, None]
    early = window / np.minimum(np.arange(PAD)[None, None, :] + 1, window)
    out["consts"] = np.concatenate([np.ones((P, P)), s == t, np.where(s <= t, 0.0, NEG), s <= t,
                                    early.reshape(P, 2 * PAD),
                                    np.broadcast_to(np.eye(NS).reshape(1, -1), (P, NS * NS))], axis=1).astype(f)
    return out


_OUTS = [("o_y", (P, KD, T)), ("o_pool_p", (L, P, 2 * 15)), ("o_pool_s", (L, P, 2 * NS * 15)), ("o_C", (L, P, NH * P)),
         ("o_n", (L, P, NH)), ("o_m", (L, NH, 1)), ("o_CT", (L, P, NS * NH * P)), ("o_nT", (L, P, NH * NS)),
         ("o_mT", (L, NH, NS)), ("o_mk", (L, P, KD * M)), ("o_mv", (L, P, 2 * D)), ("o_gv", (L, P, 2 * NS))]


def kernel(**inputs):
    import concourse.bacc as _bacc
    from concourse.bass_utils import run_bass_kernel_spmd as _run

    nc = _bacc.Bacc("TRN2", target_bir_lowering=False, num_devices=1)
    arrays = _layout(inputs)
    args = [nc.dram_tensor(n, a.shape, F32, kind="ExternalInput").ap() for n, a in arrays.items()]
    args += [nc.dram_tensor(n, shape, F32, kind="ExternalOutput").ap() for n, shape in _OUTS]
    build(nc, *args)
    r = _run(nc, [arrays], core_ids=[0]).results[0]
    y = r["o_y"].transpose(1, 0, 2).reshape(D, T).T
    pool_p = r["o_pool_p"].reshape(L, P, 2, 15).transpose(0, 3, 2, 1).reshape(L, 1, 15, 256)
    pool_s = r["o_pool_s"].reshape(L, P, 2, NS, 15).transpose(0, 3, 4, 2, 1).reshape(L, NS, 15, 256)
    C_p = r["o_C"].reshape(L, P, NH, P).transpose(0, 2, 1, 3)[:, None]
    n_p = r["o_n"].transpose(0, 2, 1)[:, None]
    m_p = r["o_m"].transpose(0, 2, 1)
    C_s = r["o_CT"].reshape(L, P, NS, NH, P).transpose(0, 2, 3, 4, 1)
    n_s = r["o_nT"].reshape(L, P, NH, NS).transpose(0, 3, 2, 1)
    m_s = r["o_mT"].transpose(0, 2, 1)
    mk = r["o_mk"].reshape(L, P, KD, M).transpose(0, 3, 2, 1).reshape(L, 1, M, NH, D // NH)
    mv = r["o_mv"].reshape(L, P, 2, D).transpose(0, 2, 1, 3).reshape(L, 1, M, NH, D // NH)
    gv = r["o_gv"].reshape(L, P, 2, NS).transpose(0, 3, 2, 1).reshape(L, NS, 1, 256)
    cut = np.ascontiguousarray
    return tuple(cut(t) for t in (y[None, :TP], y[TP:, None], pool_p, pool_s, C_p, n_p, m_p, C_s, n_s, m_s, mk, mv, gv))
```
